# Optimizing a Trainium2 kernel written in Bass

```python
import math
import jax, jax.numpy as jnp
from jax import lax
import numpy as np

D_MODEL = 1024
BATCH = 1
SEQ = 1024
DEPTH = 2

N_A_LAYERS = DEPTH // 2
N_B_LAYERS = DEPTH - N_A_LAYERS
CONV_WIDTH = 31
N_HEADS = 8
HEAD_DIM = D_MODEL // N_HEADS // 2
V_DIM = 2 * HEAD_DIM
QK_WIDTH = N_HEADS * 2 * HEAD_DIM
V_WIDTH = N_HEADS * V_DIM
D_FF = -(-(8 * D_MODEL) // (3 * 256)) * 256
Q_BLOCK = 128
EPS = 1e-6

kernel_name = "yoco_conformer_diffattn_alibi"

def rmsnorm(x, g):
    x32 = x.astype(jnp.float32)
    y = x32 * lax.rsqrt(jnp.mean(x32 * x32, axis=-1, keepdims=True) + EPS)
    return (y * g.astype(jnp.float32)).astype(x.dtype)

def layernorm(x, g, b):
    x32 = x.astype(jnp.float32)
    mu = jnp.mean(x32, axis=-1, keepdims=True)
    xc = x32 - mu
    y = xc * lax.rsqrt(jnp.mean(xc * xc, axis=-1, keepdims=True) + EPS)
    return (y * g.astype(jnp.float32) + b.astype(jnp.float32)).astype(x.dtype)

def alibi_slopes():
    return jnp.asarray((2.0 ** (-8.0 * np.arange(1, N_HEADS + 1) / N_HEADS)).astype(np.float32))

def conformer_conv(h, pw1_w, pw1_b, dw_w, dw_b, ln_g, ln_b, pw2_w, pw2_b):
    u = h @ pw1_w + pw1_b
    a, gate = jnp.split(u, 2, axis=-1)
    u = a * jax.nn.sigmoid(gate)
    u = lax.conv_general_dilated(
        u, dw_w[:, None, :].astype(u.dtype), window_strides=(1,),
        padding=((CONV_WIDTH - 1, 0),),
        dimension_numbers=("NWC", "WIO", "NWC"),
        feature_group_count=D_MODEL) + dw_b
    u = jax.nn.silu(layernorm(u, ln_g, ln_b))
    return u @ pw2_w + pw2_b

def diff_attention(h, k, v, w_q, lam_q1, lam_k1, lam_q2, lam_k2, subln_g, w_o, lambda_init):
    B, S, _ = h.shape
    q = (h @ w_q).reshape(B, S, N_HEADS, 2, HEAD_DIM)
    lam = (jnp.exp(jnp.sum(lam_q1.astype(jnp.float32) * lam_k1.astype(jnp.float32)))
           - jnp.exp(jnp.sum(lam_q2.astype(jnp.float32) * lam_k2.astype(jnp.float32)))
           + lambda_init)
    slopes = alibi_slopes()
    scale = HEAD_DIM ** -0.5
    outs = []
    for i in range(S // Q_BLOCK):
        end = (i + 1) * Q_BLOCK
        q_blk = q[:, i * Q_BLOCK:end]
        k_pre = k[:, :end]
        v_pre = v[:, :end]
        s = jnp.einsum("bqhcd,bkhcd->bhcqk", q_blk, k_pre,
                       preferred_element_type=jnp.float32) * scale
        t_pos = i * Q_BLOCK + jnp.arange(Q_BLOCK)
        s_pos = jnp.arange(end)
        dist = (t_pos[:, None] - s_pos[None, :]).astype(jnp.float32)
        bias = jnp.where(dist >= 0, -slopes[:, None, None] * dist, -jnp.inf)
        p = jax.nn.softmax(s + bias[None, :, None], axis=-1)
        attn = p[:, :, 0] - lam * p[:, :, 1]
        outs.append(jnp.einsum("bhqk,bkhe->bqhe", attn.astype(v.dtype), v_pre))
    o = jnp.concatenate(outs, axis=1)
    o = rmsnorm(o, subln_g) * (1.0 - lambda_init)
    return o.reshape(B, S, V_WIDTH) @ w_o

def swiglu(h, w1, w3, w2):
    return (jax.nn.silu(h @ w1) * (h @ w3)) @ w2

def setup_inputs(seed: int = 0) -> dict:
    key = jax.random.key(seed)
    ks = iter(jax.random.split(key, 32))
    f32 = jnp.float32

    def nrm(shape, scale):
        return jax.random.normal(next(ks), shape, f32) * scale

    def gain(shape):
        return 1.0 + nrm(shape, 0.02)

    D = D_MODEL
    return {
        "x": nrm((BATCH, SEQ, D), 1.0),
        "conv_norm_g": gain((N_A_LAYERS, D)),
        "pw1_w": nrm((N_A_LAYERS, D, 2 * D), D ** -0.5),
        "pw1_b": nrm((N_A_LAYERS, 2 * D), 0.02),
        "dw_w": nrm((N_A_LAYERS, CONV_WIDTH, D), CONV_WIDTH ** -0.5),
        "dw_b": nrm((N_A_LAYERS, D), 0.02),
        "conv_ln_g": gain((N_A_LAYERS, D)),
        "conv_ln_b": nrm((N_A_LAYERS, D), 0.02),
        "pw2_w": nrm((N_A_LAYERS, D, D), D ** -0.5),
        "pw2_b": nrm((N_A_LAYERS, D), 0.02),
        "kv_norm_g": gain((D,)),
        "w_k": nrm((D, QK_WIDTH), D ** -0.5),
        "w_v": nrm((D, V_WIDTH), D ** -0.5),
        "attn_norm_g": gain((N_B_LAYERS, D)),
        "w_q": nrm((N_B_LAYERS, D, QK_WIDTH), D ** -0.5),
        "lambda_q1": nrm((N_B_LAYERS, HEAD_DIM), 0.1),
        "lambda_k1": nrm((N_B_LAYERS, HEAD_DIM), 0.1),
        "lambda_q2": nrm((N_B_LAYERS, HEAD_DIM), 0.1),
        "lambda_k2": nrm((N_B_LAYERS, HEAD_DIM), 0.1),
        "subln_g": gain((N_B_LAYERS, V_DIM)),
        "w_o": nrm((N_B_LAYERS, V_WIDTH, D), V_WIDTH ** -0.5),
        "ffn_norm_g": gain((DEPTH, D)),
        "ffn_w1": nrm((DEPTH, D, D_FF), D ** -0.5),
        "ffn_w3": nrm((DEPTH, D, D_FF), D ** -0.5),
        "ffn_w2": nrm((DEPTH, D_FF, D), D_FF ** -0.5),
        "final_norm_g": gain((D,)),
    }

def reference(x, conv_norm_g, pw1_w, pw1_b, dw_w, dw_b, conv_ln_g, conv_ln_b, pw2_w, pw2_b,
              kv_norm_g, w_k, w_v, attn_norm_g, w_q, lambda_q1, lambda_k1, lambda_q2, lambda_k2,
              subln_g, w_o, ffn_norm_g, ffn_w1, ffn_w3, ffn_w2, final_norm_g):
    B, S, _ = x.shape
    k = None
    v = None
    for layer in range(DEPTH):
        if layer < N_A_LAYERS:
            x = x + conformer_conv(rmsnorm(x, conv_norm_g[layer]), pw1_w[layer], pw1_b[layer],
                                   dw_w[layer], dw_b[layer], conv_ln_g[layer], conv_ln_b[layer],
                                   pw2_w[layer], pw2_b[layer])
        else:
            j = layer - N_A_LAYERS
            lambda_init = 0.8 - 0.6 * math.exp(-0.3 * layer)
            x = x + diff_attention(rmsnorm(x, attn_norm_g[j]), k, v, w_q[j],
                                   lambda_q1[j], lambda_k1[j], lambda_q2[j], lambda_k2[j],
                                   subln_g[j], w_o[j], lambda_init)
        x = x + swiglu(rmsnorm(x, ffn_norm_g[layer]), ffn_w1[layer], ffn_w3[layer], ffn_w2[layer])
        if layer == N_A_LAYERS - 1:
            kv_in = rmsnorm(x, kv_norm_g)
            k = (kv_in @ w_k).reshape(B, S, N_HEADS, 2, HEAD_DIM)
            v = (kv_in @ w_v).reshape(B, S, N_HEADS, V_DIM)
    return rmsnorm(x, final_norm_g)


_drawn_inputs = setup_inputs


def setup_inputs(seed=0):
    import zlib

    import numpy as np

    out = dict(_drawn_inputs(seed))
    spreads = {}
    factors = {'conv_norm_g': 3.462,
     'pw1_b': 2.898,
     'conv_ln_g': 2.968,
     'conv_ln_b': 3.198,
     'kv_norm_g': 4.477,
     'attn_norm_g': 6.401,
     'lambda_k2': 4.003,
     'subln_g': 6.205,
     'ffn_norm_g': 2.88,
     'final_norm_g': 2.812}
    for name, (base, spread) in spreads.items():
        noise = np.random.default_rng([zlib.crc32(name.encode()), seed]).standard_normal(out[name].shape)
        drawn = base * np.exp(spread * noise) if base else spread * noise
        out[name] = __import__('jax').numpy.asarray(drawn.astype(out[name].dtype))
    for name, factor in factors.items():
        out[name] = (out[name] * factor).astype(out[name].dtype)
    return out
```

```python
import math
from contextlib import ExitStack

import concourse.bass as bass
from concourse import mybir

F32 = mybir.dt.float32
F32R = mybir.dt.float32r
ALU = mybir.AluOpType
ACT = mybir.ActivationFunctionType
AX_X = mybir.AxisListType.X

P = 128
D = 1024
T = 1024
HT = 512
KC = D // P
TB = T // P
F = 2816
FC = F // P
CW = 31
PAD = CW - 1
HEADS = 8
HD = 64
EPS = 1e-6
LAMBDA_INIT = 0.8 - 0.6 * math.exp(-0.3)
QK_SCALE = HD ** -0.5
MASKED = -1e37
ACT_TAPS = 10
DVE_TAPS = CW - ACT_TAPS

RING = 4
GROUP = 6
GROUPS = FC // GROUP
REST = FC - GROUP * GROUPS
GROUP_TURNS = 2 * GROUP // RING + KC // RING
REST_TURNS = 2 * REST // RING + KC // RING
FFN_TURNS = GROUPS * GROUP_TURNS + REST_TURNS
TURN_PW1 = 0
TURN_PW2 = TURN_PW1 + 2 * KC // RING
TURN_FFN0 = TURN_PW2 + KC // RING
TURN_ATT = TURN_FFN0 + FFN_TURNS
TURN_FFN1 = TURN_ATT + HEADS
TURNS = TURN_FFN1 + FFN_TURNS

VECS = {}
for _name, _rows in (("conv_norm_g", KC), ("pw1_b", 2 * KC), ("dw_b", KC), ("conv_ln_g", KC), ("conv_ln_b", KC),
                     ("pw2_b", KC), ("ffn_norm_g", 2 * KC), ("kv_norm_g", KC), ("attn_norm_g", KC),
                     ("final_norm_g", KC), ("subln_g", 1)):
    VECS[_name] = (sum(r for _, r in VECS.values()), _rows)
NVEC = sum(r for _, r in VECS.values())
DWR = CW * KC // 2

KB = 1024
X_AT = 0
S_AT = 32 * KB
G_AT = S_AT + 64 * KB
RAW_AT = G_AT + 48 * KB
W_AT = RAW_AT + 8 * KB
RSTD_AT = W_AT + 32 * KB
R_AT = RSTD_AT + 4 * KB
SMALL_AT = R_AT + 16 * KB


def trunk(nc, a, out):
    with ExitStack() as ctx:
        base = -(-nc.sbuf_base // 64) * 64

        def at(name, shape, dt, offset):
            return nc.alloc_sbuf_tensor_at(name, shape, dt, offset=base + offset)

        def sem(name):
            return ctx.enter_context(nc.semaphore(name))

        xT = at("xT", [P, KC, T], F32, X_AT)
        Sh = at("Sh", [P, KC, T], F32R, S_AT)
        Sl = at("Sl", [P, KC, T], F32R, S_AT + 32 * KB)
        yout = at("yout", [P, TB, D], F32, S_AT)
        Gh = at("Gh", [P, GROUP, T], F32R, G_AT)
        Gl = at("Gl", [P, GROUP, T], F32R, G_AT + 24 * KB)
        xrow = at("xrow", [P, TB, D], F32, G_AT)
        vrow = at("vrow", [P, P], F32, G_AT + 32 * KB)
        dwrow = at("dwrow", [DWR, 2, P], F32, G_AT + 33 * KB)
        lamv = at("lamv", [P, 4, HD], F32, G_AT + 34 * KB)
        cv = at("cv", [P, KC, T], F32, G_AT)
        up = at("up", [P, 2, PAD + T + 2], F32, G_AT + 32 * KB)
        cacc = at("cacc", [P, T], F32, G_AT + 41 * KB)
        prod = at("prod", [P, T], F32, R_AT + 4 * KB)
        ATh = at("ATh", [P, TB, 2 * P], F32R, G_AT)
        ATl = at("ATl", [P, TB, 2 * P], F32R, G_AT + 8 * KB)
        Qh = at("Qh", [P, T], F32R, G_AT + 16 * KB)
        Ql = at("Ql", [P, T], F32R, G_AT + 20 * KB)
        Kh = at("Kh", [P, T], F32R, G_AT + 24 * KB)
        Kl = at("Kl", [P, T], F32R, G_AT + 28 * KB)
        Vh = at("Vh", [P, TB, P], F32R, G_AT + 32 * KB)
        Vl = at("Vl", [P, TB, P], F32R, G_AT + 36 * KB)
        Oh = at("Oh", [P, T], F32R, G_AT + 40 * KB)
        Ol = at("Ol", [P, T], F32R, G_AT + 44 * KB)
        raw = [at(f"raw{r}", [P, KC, P], F32, RAW_AT + r * 4 * KB) for r in range(2)]
        Wh = [at(f"Wh{r}", [P, KC, P], F32R, W_AT + r * 8 * KB) for r in range(RING)]
        Wl = [at(f"Wl{r}", [P, KC, P], F32R, W_AT + r * 8 * KB + 4 * KB) for r in range(RING)]
        rstd = at("rstd", [P, T], F32, RSTD_AT)
        acc = at("acc", [P, T], F32, R_AT)
        sq = at("sq", [P, T], F32, R_AT + 4 * KB)
        tmp = at("tmp", [P, 2, 2, HT], F32, R_AT + 8 * KB)
        mu = at("mu", [P, T], F32, R_AT + 8 * KB)
        vT = at("vT", [P, T], F32, R_AT)
        bias = at("bias", [P, T], F32, R_AT + 4 * KB)
        sc = at("sc", [P, 2, T], F32, R_AT + 8 * KB)
        ident = at("ident", [P, P], F32, SMALL_AT)
        ones = at("ones", [P, P], F32, SMALL_AT + 512)
        vec = at("vec", [P, NVEC], F32, SMALL_AT + 1024)
        dw = at("dw", [P, 2 * DWR], F32, SMALL_AT + 1024 + 480)
        small = at("small", [P, 32], F32, SMALL_AT + 1024 + 480 + 1024)
        eps = small[:, 0:1]
        neg_lam = small[:, 1:2]
        sub_g = small[:, 2:3]
        lsum = small[:, 4:6]
        lexp = small[:, 6:8]
        negmax = small[:, 8:10]
        rowsum = small[:, 10:12]
        rrow = small[:, 12:14]
        rlam = small[:, 14:15]
        lpair = at("lpair", [P, 2, HD], F32, G_AT + 35 * KB)
        ps = nc.alloc_psum_tensor("ps", [P, 8, HT], F32)

        def col(name, k=0):
            return vec[:, bass.ds(VECS[name][0] + k, 1)]

        consts = sem("consts")
        vec_in = sem("vec_in")
        x_in = [sem(f"x_in{t}") for t in range(TB)]
        vec_t = sem("vec_t")
        vec_ev = sem("vec_ev")
        xt_mm = sem("xt_mm")
        xt_ev = sem("xt_ev")
        lam_s = sem("lam_s")
        lam_e = sem("lam_e")
        raw_in = [sem(f"raw_in{r}") for r in range(2)]
        raw_ok = sem("raw_ok")
        w_hi = sem("w_hi")
        w_lo = sem("w_lo")
        mm = sem("mm")
        rel = sem("rel")
        s_hi = sem("s_hi")
        s_lo = sem("s_lo")
        sq_ok = sem("sq_ok")
        acc_ok = sem("acc_ok")
        var_mm = sem("var_mm")
        std_ok = sem("std_ok")
        rstd_ok = sem("rstd_ok")
        gate_t = sem("gate_t")
        gate_s = sem("gate_s")
        val_t = sem("val_t")
        glu_ok = sem("glu_ok")
        prod_ok = sem("prod_ok")
        tap_ok = sem("tap_ok")
        conv_s = sem("conv_s")
        cv_ok = sem("cv_ok")
        mean_mm = sem("mean_mm")
        mu_ok = sem("mu_ok")
        xc_ok = sem("xc_ok")
        ln_t = sem("ln_t")
        ln_y = sem("ln_y")
        x_ok = sem("x_ok")
        t1_ok = sem("t1_ok")
        silu_ok = sem("silu_ok")
        t3_ok = sem("t3_ok")
        hid_t = sem("hid_t")
        hid_hi = sem("hid_hi")
        hid_lo = sem("hid_lo")
        bias_ok = sem("bias_ok")
        pj_t = sem("pj_t")
        pj_hi = sem("pj_hi")
        qk_lo = sem("qk_lo")
        pj_ev = sem("pj_ev")
        vt_mm = sem("vt_mm")
        v_hi = sem("v_hi")
        v_lo = sem("v_lo")
        s_mm = sem("s_mm")
        s_ev = sem("s_ev")
        e_ok = sem("e_ok")
        att_s = sem("att_s")
        a_ok = sem("a_ok")
        tr_mm = sem("tr_mm")
        at_hi = sem("at_hi")
        tr_ev = sem("tr_ev")
        pv_mm = sem("pv_mm")
        osq_ok = sem("osq_ok")
        ov_mm = sem("ov_mm")
        ostd_ok = sem("ostd_ok")
        orec_ok = sem("orec_ok")
        o_hi = sem("o_hi")
        o_lo = sem("o_lo")
        wo_mm = sem("wo_mm")
        wo_ev = sem("wo_ev")
        y_ok = sem("y_ok")
        yt_mm = sem("yt_mm")
        yt_ev = sem("yt_ev")
        went_on = sem("went_on")
        stored = sem("stored")

        block = ctx.enter_context(nc.Block())

        def apart(eng):
            eng.sem_inc(went_on, 1)

        def flat(ap):
            return ap.rearrange("p a b -> p (a b)")

        def n_block(turn, s):
            return turn * RING + s + 1

        def n_half(turn, s, hf):
            return turn * (2 * RING) + (2 * s + hf + 1)

        def n_rel(turn, s):
            return turn * RING + s + 1

        w1, w3, w2 = a["ffn_w1"], a["ffn_w3"], a["ffn_w2"]

        @block.sync
        def _(sp):
            for n, (name, (at0, rows)) in enumerate(VECS.items()):
                src = a[name]
                flat_src = src.rearrange("a (r p) -> (a r) p", p=P) if len(src.shape) == 2 else \
                    src.rearrange("(r p) -> r p", p=P)
                sp.dma_start(vrow[at0:at0 + rows, :], flat_src).then_inc(vec_in, 16)
            sp.dma_start(dwrow[:, :, :], a["dw_w"][0].rearrange("j (c p) -> (j c) p", p=P)
                         .rearrange("(s q) p -> q s p", s=2)).then_inc(vec_in, 16)
            for n, name in enumerate(("lambda_q1", "lambda_k1", "lambda_q2", "lambda_k2")):
                sp.dma_start(lamv[:, n, :], a[name].broadcast_to([P, HD])).then_inc(vec_in, 16)
            xin = a["x"][0].rearrange("(t p) d -> t p d", p=P)
            for t in range(2):
                sp.dma_start(xrow[:, t, :], xin[t]).then_inc(x_in[t], 16)

            def load(turn, s, src, first=False):
                if not first:
                    sp.wait_ge(w_lo, turn * RING + (s - 1))
                sp.dma_start(raw[s % 2][:, 0:src.shape[1], :] if len(src.shape) == 3 else flat(raw[s % 2]),
                             src).then_inc(raw_in[s % 2], 16)

            pw1 = a["pw1_w"][0].rearrange("(k p) n -> p k n", p=P)
            pw2 = a["pw2_w"][0].rearrange("(k p) n -> p k n", p=P)

            def pw1_turn(i, first=False):
                for s in range(RING):
                    c0 = (2 * i + s // 2) * P + (s % 2) * D
                    load(TURN_PW1 + i, s, pw1[:, :, bass.ds(c0, P)], first and s < 2)
                    if first and s == 1:
                        for t in range(2, TB):
                            sp.dma_start(xrow[:, t, :], xin[t]).then_inc(x_in[t], 16)

            pw1_turn(0, True)
            with sp.Fori(1, 2 * KC // RING) as i:
                pw1_turn(i)
            with sp.Fori(0, KC // RING) as i:
                for s in range(RING):
                    load(TURN_PW2 + i, s, pw2[:, :, bass.ds((RING * i + s) * P, P)])

            def ffn(layer, turn0):
                u1 = w1[layer].rearrange("(k p) n -> p k n", p=P)
                u3 = w3[layer].rearrange("(k p) n -> p k n", p=P)
                u2 = w2[layer].rearrange("(k p) n -> p k n", p=P)

                def group(g, size, turn):
                    with sp.Fori(0, size // 2) as i:
                        for s in range(RING):
                            c0 = (g * GROUP + 2 * i + s // 2) * P
                            load(turn + i, s, (u3 if s % 2 else u1)[:, :, bass.ds(c0, P)])
                    with sp.Fori(0, KC // RING) as i:
                        for s in range(RING):
                            load(turn + size // 2 + i, s,
                                 u2[:, bass.ds(g * GROUP, size), bass.ds((RING * i + s) * P, P)])

                with sp.Fori(0, GROUPS) as g:
                    group(g, GROUP, turn0 + g * GROUP_TURNS)
                group(GROUPS, REST, turn0 + GROUPS * GROUP_TURNS)

            ffn(0, TURN_FFN0)
            wq = a["w_q"][0].rearrange("(k p) n -> p k n", p=P)
            wk = a["w_k"].rearrange("(k p) n -> p k n", p=P)
            wv = a["w_v"].rearrange("(k p) n -> p k n", p=P)
            with sp.Fori(0, HEADS) as h:
                for s, w in enumerate((wq, wk, wv)):
                    load(TURN_ATT + h, s, w[:, :, bass.ds(h * P, P)])
                load(TURN_ATT + h, 3, a["w_o"][0][bass.ds(h * P, P), :])
            ffn(1, TURN_FFN1)

            for t in range(TB):
                sp.wait_ge(yt_ev, t + 1)
                sp.dma_start(out[0, t * P:(t + 1) * P, :], yout[:, t, :]).then_inc(stored, 16)
            sp.wait_ge(stored, 16 * TB)

        @block.gpsimd
        def _(pool):
            pool.memset(ident[:, :], 0.0).then_inc(consts, 1)
            pool.memset(ones[:, :], 1.0).then_inc(consts, 1)
            pool.memset(eps, EPS).then_inc(consts, 1)
            pool.wait_ge(consts, 1)
            pool.affine_select(out=ident[:, :], in_=ident[:, :], compare_op=ALU.not_equal, fill=1.0, base=0,
                               pattern=[[-1, P]], channel_multiplier=1).then_inc(consts, 1)

            def passed(turn, s, gain=None):
                pool.wait_ge(raw_in[s % 2], turn * 32 + 16 * (s // 2 + 1))
                if gain is None:
                    pool.sem_inc(raw_ok, 1)
                else:
                    at0 = VECS[gain][0]
                    g = vec[:, at0:at0 + KC].unsqueeze(2).to_broadcast([P, KC, P])
                    r = raw[s % 2][:, :, :]
                    pool.tensor_tensor(r, r, g, ALU.mult).then_inc(raw_ok, 1)
                    pool.wait_ge(raw_ok, n_block(turn, s))

            def pass_turns(turn0, turns):
                with pool.Fori(0, turns) as i:
                    for s in range(RING):
                        passed(turn0 + i, s)

            def sum_squares(n):
                if n:
                    pool.wait_ge(var_mm, 2 * n)
                pool.memset(acc[:, :], 0.0).then_inc(acc_ok, 1)
                with pool.Fori(0, KC) as k:
                    pool.wait_ge(sq_ok, k + (KC * n + 1))
                    pool.wait_ge(acc_ok, k + ((KC + 1) * n + 1))
                    pool.tensor_tensor(acc[:, :], acc[:, :], sq[:, :], ALU.add).then_inc(acc_ok, 1)
                pool.wait_ge(acc_ok, (KC + 1) * (n + 1))

            passed(TURN_PW1, 0)
            passed(TURN_PW1, 1)
            sum_squares(0)
            passed(TURN_PW1, 2)
            passed(TURN_PW1, 3)

            def conv_taps(n):
                for j in range(1, ACT_TAPS):
                    pool.wait_ge(prod_ok, n * ACT_TAPS + (j + 1))
                    if j > 1:
                        pool.wait_ge(tap_ok, n * (ACT_TAPS - 1) + (j - 1))
                    pool.tensor_tensor(cacc[:, :], cacc[:, :], prod[:, :], ALU.add).then_inc(tap_ok, 1)

            with pool.Fori(0, KC // 2 - 1) as i:
                passed(i + 1, 0)
                passed(i + 1, 1)
                conv_taps(2 * i)
                passed(i + 1, 2)
                passed(i + 1, 3)
                conv_taps(2 * i + 1)
            passed(TURN_PW2, 0)
            passed(TURN_PW2, 1)
            conv_taps(KC - 2)
            conv_taps(KC - 1)
            sum_squares(1)
            passed(TURN_PW2, 2)
            passed(TURN_PW2, 3)
            pass_turns(TURN_PW2 + 1, 1)
            passed(TURN_FFN0, 0)
            passed(TURN_FFN0, 1)
            sum_squares(2)
            passed(TURN_FFN0, 2)
            passed(TURN_FFN0, 3)
            pass_turns(TURN_FFN0 + 1, FFN_TURNS - 1)

            passed(TURN_ATT, 0, "attn_norm_g")
            passed(TURN_ATT, 1, "kv_norm_g")
            sum_squares(3)
            bt = bias[:, :]
            pool.iota(bt, pattern=[[1, T]], base=-(T - P), channel_multiplier=-1,
                      allow_small_or_imprecise_dtypes=True).then_inc(bias_ok, 1)
            pool.wait_ge(bias_ok, 1)
            pool.tensor_scalar(bt, bt, 1.0 / QK_SCALE, 0.0, ALU.mult, ALU.add).then_inc(bias_ok, 1)
            pool.wait_ge(bias_ok, 2)
            pool.affine_select(out=bt, in_=bt, compare_op=ALU.is_ge, fill=MASKED, base=T - P,
                               pattern=[[-1, T]], channel_multiplier=1).then_inc(bias_ok, 1)

            def head_bias(h):
                pool.wait_ge(s_ev, h * (2 * TB) + 2)
                pool.wait_ge(bias_ok, h + 3)
                apart(pool)
                pool.tensor_scalar(bt, bt, 0.5, 0.0, ALU.mult, ALU.add).then_inc(bias_ok, 1)

            head_bias(0)
            passed(TURN_ATT, 2, "kv_norm_g")
            passed(TURN_ATT, 3)
            with pool.Fori(1, HEADS) as h:
                passed(TURN_ATT + h, 0, "attn_norm_g")
                passed(TURN_ATT + h, 1, "kv_norm_g")
                head_bias(h)
                passed(TURN_ATT + h, 2, "kv_norm_g")
                passed(TURN_ATT + h, 3)
            passed(TURN_FFN1, 0)
            passed(TURN_FFN1, 1)
            pool.wait_ge(wo_ev, HEADS * 16 + 4)
            sum_squares(4)
            passed(TURN_FFN1, 2)
            passed(TURN_FFN1, 3)
            pass_turns(TURN_FFN1 + 1, FFN_TURNS - 1)
            sum_squares(5)

        @block.scalar
        def _(act):
            def squares(n, k, src):
                act.wait_ge(acc_ok, k + ((KC + 1) * n + 1))
                apart(act)
                act.activation(sq[:, :], src, ACT.Square).then_inc(sq_ok, 1)

            def root(n):
                for hf in range(2):
                    act.wait_ge(var_mm, 2 * n + hf + 1)
                    act.activation(rstd[:, hf * HT:(hf + 1) * HT], ps[:, var_bank[n] + hf, :], ACT.Sqrt, bias=eps,
                                   scale=1.0 / D).then_inc(std_ok, 1)

            def renorm(n, x_base, hi_base, gain, gain_at=0):
                with act.Fori(0, KC) as k:
                    if x_base is not None:
                        act.wait_ge(x_ok, k + (x_base + 1))
                        apart(act)
                    act.activation(Sh[:, k, :], xT[:, k, :], ACT.Copy,
                                   scale=1.0 if gain is None else col(gain, gain_at + k)).then_inc(s_hi, 1)
                    squares(n, k, xT[:, k, :])
                root(n)

            for t in range(TB):
                act.wait_ge(xt_mm, t + 1)
                act.activation(xT[:, :, t * P:(t + 1) * P],
                               ps[:, 2 * (t % 4):2 * (t % 4) + 2, :].rearrange("p b (c q) -> p (b c) q", q=P),
                               ACT.Copy).then_inc(xt_ev, 1)
                if t == 0:
                    act.wait_ge(lam_s, 2)
                    act.activation(lexp, lsum, ACT.Exp).then_inc(lam_e, 1)
            act.wait_ge(raw_ok, 1)
            act.activation(flat(Wh[0]), flat(raw[0]), ACT.Copy).then_inc(w_hi, 1)
            act.wait_ge(raw_ok, 2)
            act.activation(flat(Wh[1]), flat(raw[1]), ACT.Copy).then_inc(w_hi, 1)
            act.wait_ge(vec_ev, 3)
            act.wait_ge(xt_ev, TB)
            renorm(0, None, 0, "conv_norm_g")

            def pw1_pair(turn, n, cc, next_turn, first=False):
                for s in (0, 1):
                    b = 2 * cc + s + 2
                    if first and b < RING:
                        act.wait_ge(raw_ok, b + 1)
                        act.activation(flat(Wh[b]), flat(raw[b % 2]), ACT.Copy).then_inc(w_hi, 1)
                    else:
                        w_split(turn, 2 * cc + s)
                for hf in range(2):
                    act.wait_ge(gate_t, n * 2 + (hf + 1))
                    apart(act)
                    act.activation(tmp[:, hf, 0, :], tmp[:, hf, 0, :], ACT.Sigmoid,
                                   bias=col("pw1_b", KC + n)).then_inc(gate_s, 1)
                act.wait_ge(glu_ok, n * 2 + 3)
                for j in range(ACT_TAPS):
                    if j == 0:
                        if not (first and cc == 0):
                            act.wait_ge(cv_ok, n)
                        dst = cacc
                    else:
                        if j == 1 and not (first and cc == 0):
                            act.wait_ge(tap_ok, n * (ACT_TAPS - 1))
                        if j > 1:
                            act.wait_ge(tap_ok, n * (ACT_TAPS - 1) + (j - 1))
                        dst = prod
                    act.activation(dst[:, :], up[:, cc, j:j + T], ACT.Copy,
                                   scale=dw[:, bass.ds(j * KC + n, 1)]).then_inc(prod_ok, 1)

            def w_split(turn, s):
                t2, s2 = turn + (s + 2) // RING, (s + 2) % RING
                act.wait_ge(raw_ok, n_block(t2, s2))
                act.wait_ge(mm, n_half(t2, s2, 1) - 2 * RING)
                act.activation(flat(Wh[s2]), flat(raw[s2 % 2]), ACT.Copy).then_inc(w_hi, 1)

            for cc in range(2):
                pw1_pair(0, cc, cc, 1, True)
            with act.Fori(1, KC // 2) as i:
                for cc in range(2):
                    pw1_pair(i, 2 * i + cc, cc, i + 1)

            for hf in range(2):
                act.wait_ge(mean_mm, hf + 1)
                act.activation(mu[:, hf * HT:(hf + 1) * HT], ps[:, hf, :], ACT.Copy, scale=1.0 / D).then_inc(mu_ok, 1)
            with act.Fori(0, KC) as k:
                act.wait_ge(xc_ok, k + 1)
                squares(1, k, cv[:, k, :])
            root(1)
            with act.Fori(0, KC) as k:
                act.wait_ge(ln_t, k + 1)
                apart(act)
                act.activation(cv[:, k, :], cv[:, k, :], ACT.Silu, bias=col("conv_ln_b", k),
                               scale=col("conv_ln_g", k)).then_inc(ln_y, 1)
                act.wait_ge(ln_y, k + 1)
                apart(act)
                act.activation(Sh[:, k, :], cv[:, k, :], ACT.Copy).then_inc(s_hi, 1)

            with act.Fori(0, KC // RING) as i:
                for s in range(RING):
                    w_split(TURN_PW2 + i, s)
            act.wait_ge(mm, n_half(TURN_FFN0 - 1, RING - 1, 1))
            renorm(2, 0, 2 * KC, "ffn_norm_g", 0)

            def ffn(layer, turn0):
                def group(g, size, turn):
                    with act.Fori(0, size // 2) as i:
                        for cc in range(2):
                            for s in range(2):
                                w_split(turn + i, 2 * cc + s)
                            m = (g * GROUP + 2 * i + cc) * 2 + 2 * FC * layer
                            for hf in range(2):
                                act.wait_ge(t1_ok, m + (hf + 1))
                                act.activation(tmp[:, hf, 0, :], tmp[:, hf, 0, :], ACT.Silu).then_inc(silu_ok, 1)
                            for hf in range(2):
                                act.wait_ge(hid_t, m + (hf + 1))
                                apart(act)
                                act.activation(Gh[:, 2 * i + cc, hf * HT:(hf + 1) * HT], tmp[:, hf, 1, :],
                                               ACT.Copy).then_inc(hid_hi, 1)

                    def down(i, splits):
                        for s in range(splits):
                            w_split(turn + size // 2 + i, s)

                    if layer == 1 and size == REST:
                        for i in range(KC // RING):
                            down(i, RING if i + 1 < KC // RING else RING - 2)
                    else:
                        with act.Fori(0, KC // RING) as i:
                            down(i, RING)

                with act.Fori(0, GROUPS) as g:
                    group(g, GROUP, turn0 + g * GROUP_TURNS)
                group(GROUPS, REST, turn0 + GROUPS * GROUP_TURNS)

            ffn(0, TURN_FFN0)
            renorm(3, KC, 3 * KC, None)

            with act.Fori(0, HEADS) as h:
                turn = TURN_ATT + h
                for s, (dst, base) in enumerate(((Qh, 0), (Kh, 2))):
                    w_split(turn, s)
                    for hf in range(2):
                        act.wait_ge(pj_t, h * 4 + (base + hf + 1))
                        act.activation(dst[:, hf * HT:(hf + 1) * HT], sc[:, 0, hf * HT:(hf + 1) * HT],
                                       ACT.Copy).then_inc(pj_hi, 1)
                w_split(turn, 2)
                for hf in range(2):
                    act.wait_ge(vt_mm, h * 2 + (hf + 1))
                    act.activation(flat(Vh[:, 4 * hf:4 * hf + 4, :]), ps[:, 6 + hf, :], ACT.Copy).then_inc(v_hi, 1)
                g = 0
                for i in range(TB):
                    w = (i + 1) * P
                    for c in range(2):
                        act.wait_ge(s_ev, h * (2 * TB) + (2 * i + c + 3))
                        act.activation(sc[:, c, 0:w], sc[:, c, 0:w], ACT.Exp, bias=negmax[:, c:c + 1], scale=-1.0,
                                       accum_out=rowsum[:, c:c + 1]).then_inc(e_ok, 1)
                    if i % 2 == 0:
                        if i:
                            act.wait_ge(pv_mm, h * 4 + i // 2)
                    for j0 in range(0, i + 1, 4):
                        nj = min(4, i + 1 - j0)
                        act.wait_ge(tr_mm, h * 12 + (g + 1))
                        act.activation(ATh[:, j0:j0 + nj, (i % 2) * P:(i % 2 + 1) * P],
                                       ps[:, 6 + g % 2, 0:nj * P].rearrange("p (j q) -> p j q", q=P),
                                       ACT.Copy).then_inc(at_hi, 1)
                        g += 1
                w_split(turn, 3)
                for hf in range(2):
                    act.wait_ge(pv_mm, h * 4 + (2 * hf + 2))
                    act.activation(vT[:, hf * HT:(hf + 1) * HT], ps[:, hf, :], ACT.Square).then_inc(osq_ok, 1)
                for hf in range(2):
                    act.wait_ge(ov_mm, h * 2 + (hf + 1))
                    act.activation(sc[:, 1, hf * HT:(hf + 1) * HT], ps[:, 4 + hf, :], ACT.Sqrt, bias=eps,
                                   scale=1.0 / P).then_inc(ostd_ok, 1)
                for hf in range(2):
                    act.wait_ge(pj_ev, h * 8 + (6 + hf + 3))
                    act.activation(Oh[:, hf * HT:(hf + 1) * HT], vT[:, hf * HT:(hf + 1) * HT], ACT.Copy,
                                   scale=sub_g).then_inc(o_hi, 1)
            act.wait_ge(mm, n_half(TURN_FFN1 - 1, RING - 1, 1))
            act.wait_ge(wo_ev, HEADS * 16 + 4)
            renorm(4, None, 4 * KC, "ffn_norm_g", KC)
            ffn(1, TURN_FFN1)

            with act.Fori(0, KC) as k:
                act.wait_ge(x_ok, k + (2 * KC + 1))
                squares(5, k, xT[:, k, :])
            root(5)
            for t in range(TB):
                act.wait_ge(yt_mm, t + 1)
                act.activation(yout[:, t, :], flat(ps[:, 2 * (t % 4):2 * (t % 4) + 2, :]),
                               ACT.Copy).then_inc(yt_ev, 1)

        @block.vector
        def _(dve):
            dve.sem_inc(rel, RING)
            dve.sem_inc(pj_ev, 2)
            dve.sem_inc(s_ev, 2)
            dve.sem_inc(tr_ev, 2)
            dve.sem_inc(wo_ev, 4)

            def w_lo_of(turn, s):
                t2, s2 = turn + (s + 2) // RING, (s + 2) % RING
                dve.wait_ge(w_hi, n_block(t2, s2))
                dve.tensor_tensor(flat(Wl[s2]), flat(raw[s2 % 2]), flat(Wh[s2]).bitcast(F32),
                                  ALU.subtract).then_inc(w_lo, 1)

            def recip(n):
                for hf in range(2):
                    v = rstd[:, hf * HT:(hf + 1) * HT]
                    dve.wait_ge(std_ok, 2 * n + hf + 1)
                    dve.reciprocal(v, v).then_inc(rstd_ok, 1)
                dve.wait_ge(rstd_ok, 2 * n + 2)

            def renorm(n, base, gain, gain_at=0):
                with dve.Fori(0, KC) as k:
                    dve.wait_ge(s_hi, k + (base + 1))
                    g = 1.0 if gain is None else col(gain, gain_at + k)
                    dve.scalar_tensor_tensor(Sl[:, k, :], xT[:, k, :], g, Sh[:, k, :].bitcast(F32),
                                             ALU.mult, ALU.subtract).then_inc(s_lo, 1)
                recip(n)

            dve.wait_ge(vec_t, 3)
            dve.tensor_copy(vec[:, :], ps[:, 6, 0:NVEC]).then_inc(vec_ev, 1)
            dve.tensor_copy(dw[:, 0:DWR], ps[:, 7, 0:DWR]).then_inc(vec_ev, 1)
            dve.tensor_copy(dw[:, DWR:2 * DWR], ps[:, 7, P:P + DWR]).then_inc(vec_ev, 1)
            dve.wait_ge(vec_in, 16 * (len(VECS) + 5))
            dve.tensor_tensor(lpair[:, :, :], lamv[:, 0:4:2, :], lamv[:, 1:4:2, :], ALU.mult).then_inc(lam_s, 1)
            dve.wait_ge(lam_s, 1)
            dve.tensor_reduce(lsum, lpair[:, :, :], AX_X, ALU.add).then_inc(lam_s, 1)
            dve.wait_ge(lam_e, 1)
            dve.tensor_tensor(neg_lam, lexp[:, 1:2], lexp[:, 0:1], ALU.subtract).then_inc(lam_s, 1)
            dve.wait_ge(lam_s, 3)
            dve.tensor_scalar(neg_lam, neg_lam, -LAMBDA_INIT, None, ALU.add).then_inc(lam_s, 1)
            dve.wait_ge(vec_ev, 3)
            dve.tensor_scalar(sub_g, col("subln_g"), 1.0 - LAMBDA_INIT, None, ALU.mult).then_inc(lam_s, 1)
            for b in range(2):
                dve.wait_ge(w_hi, b + 1)
                dve.tensor_tensor(flat(Wl[b]), flat(raw[b]), flat(Wh[b]).bitcast(F32), ALU.subtract).then_inc(w_lo, 1)
            renorm(0, 0, "conv_norm_g")

            dve.memset(up[:, :, 0:PAD], 0.0).then_inc(glu_ok, 1)

            PER = DVE_TAPS + 1
            def pw1_pair(turn, n, cc):
                w_lo_of(turn, 2 * cc)
                w_lo_of(turn, 2 * cc + 1)
                val, gate = 4 * cc, 4 * cc + 2
                for hf in range(2):
                    dve.wait_ge(mm, n_half(turn, 2 * cc + 1, hf))
                    r = rstd[:, hf * HT:(hf + 1) * HT]
                    dve.tensor_tensor(tmp[:, hf, 0, :], ps[:, gate + hf, :], r, ALU.mult).then_inc(gate_t, 1)
                    dve.tensor_tensor(tmp[:, hf, 1, :], ps[:, val + hf, :], r, ALU.mult).then_inc(val_t, 1)
                for hf in range(2):
                    dve.wait_ge(val_t, n * 2 + (hf + 1))
                    dve.wait_ge(gate_s, n * 2 + (hf + 1))
                    dve.scalar_tensor_tensor(up[:, cc, PAD + hf * HT:PAD + (hf + 1) * HT], tmp[:, hf, 1, :],
                                             col("pw1_b", n), tmp[:, hf, 0, :], ALU.add, ALU.mult).then_inc(glu_ok, 1)
                dve.sem_inc(rel, 2)
                dve.wait_ge(glu_ok, n * 2 + 3)
                o = cv[:, n, :]
                for m in range(DVE_TAPS):
                    j = ACT_TAPS + m
                    wj = dw[:, bass.ds(j * KC + n, 1)]
                    src = up[:, cc, j:j + T]
                    if m == 0:
                        dve.tensor_scalar(o, src, wj, col("dw_b", n), ALU.mult, ALU.add).then_inc(conv_s, 1)
                    else:
                        dve.wait_ge(conv_s, n * DVE_TAPS + m)
                        dve.scalar_tensor_tensor(o, src, wj, o, ALU.mult, ALU.add).then_inc(conv_s, 1)
                dve.wait_ge(conv_s, n * DVE_TAPS + DVE_TAPS)
                dve.wait_ge(tap_ok, n * (ACT_TAPS - 1) + (ACT_TAPS - 1))
                dve.tensor_tensor(o, o, cacc[:, :], ALU.add).then_inc(cv_ok, 1)

            with dve.Fori(0, KC // 2) as i:
                for cc in range(2):
                    pw1_pair(i, 2 * i + cc, cc)

            dve.wait_ge(mu_ok, 2)
            dve.wait_ge(cv_ok, KC)
            with dve.Fori(0, KC) as k:
                dve.tensor_tensor(cv[:, k, :], cv[:, k, :], mu[:, :], ALU.subtract).then_inc(xc_ok, 1)
            recip(1)
            with dve.Fori(0, KC) as k:
                dve.wait_ge(xc_ok, k + 1)
                dve.tensor_tensor(cv[:, k, :], cv[:, k, :], rstd[:, :], ALU.mult).then_inc(ln_t, 1)
            with dve.Fori(0, KC) as k:
                dve.wait_ge(s_hi, k + (KC + 1))
                dve.tensor_tensor(Sl[:, k, :], cv[:, k, :], Sh[:, k, :].bitcast(F32), ALU.subtract).then_inc(s_lo, 1)

            with dve.Fori(0, KC // RING) as i:
                for s in range(RING):
                    w_lo_of(TURN_PW2 + i, s)
                    n = RING * i + s
                    for hf in range(2):
                        xs = xT[:, n, hf * HT:(hf + 1) * HT]
                        dve.wait_ge(mm, n_half(TURN_PW2 + i, s, hf))
                        ins = dve.scalar_tensor_tensor(xs, ps[:, 2 * s + hf, :], col("pw2_b", n), xs, ALU.add, ALU.add)
                    ins.then_inc(x_ok, 1)
                    dve.wait_ge(x_ok, n + 1)
                    dve.sem_inc(rel, 1)
            renorm(2, 2 * KC, "ffn_norm_g", 0)

            def ffn(layer, turn0, x_base):
                def group(g, size, turn, last):
                    with dve.Fori(0, size // 2) as i:
                        for cc in range(2):
                            b1, b3 = 4 * cc, 4 * cc + 2
                            m = (g * GROUP + 2 * i + cc) * 2 + 2 * FC * layer
                            w_lo_of(turn + i, 2 * cc)
                            for hf in range(2):
                                dve.wait_ge(mm, n_half(turn + i, 2 * cc, hf))
                                dve.tensor_tensor(tmp[:, hf, 0, :], ps[:, b1 + hf, :], rstd[:, hf * HT:(hf + 1) * HT],
                                                  ALU.mult).then_inc(t1_ok, 1)
                            w_lo_of(turn + i, 2 * cc + 1)

                            def lo(hf):
                                cs = slice(hf * HT, (hf + 1) * HT)
                                dve.wait_ge(hid_hi, m + (hf + 1))
                                dve.tensor_tensor(Gl[:, 2 * i + cc, cs], tmp[:, hf, 1, :],
                                                  Gh[:, 2 * i + cc, cs].bitcast(F32), ALU.subtract).then_inc(hid_lo, 1)

                            for hf in range(2):
                                dve.wait_ge(mm, n_half(turn + i, 2 * cc + 1, hf))
                                dve.tensor_tensor(tmp[:, hf, 1, :], ps[:, b3 + hf, :], rstd[:, hf * HT:(hf + 1) * HT],
                                                  ALU.mult).then_inc(t3_ok, 1)
                                dve.wait_ge(t3_ok, m + (hf + 1))
                                dve.wait_ge(silu_ok, m + (hf + 1))
                                dve.tensor_tensor(tmp[:, hf, 1, :], tmp[:, hf, 1, :], tmp[:, hf, 0, :],
                                                  ALU.mult).then_inc(hid_t, 1)
                                if hf:
                                    dve.sem_inc(rel, 2)
                                    lo(0)
                            lo(1)
                            dve.wait_ge(hid_lo, m + 2)

                    def down(i, splits):
                        for s in range(RING):
                            if s < splits:
                                w_lo_of(turn + size // 2 + i, s)
                            n = RING * i + s
                            for hf in range(2):
                                xs = xT[:, n, hf * HT:(hf + 1) * HT]
                                dve.wait_ge(mm, n_half(turn + size // 2 + i, s, hf))
                                ins = dve.tensor_tensor(xs, ps[:, 2 * s + hf, :], xs, ALU.add)
                                if hf:
                                    ins.then_inc(x_ok if last else rel, 1)
                            if last:
                                dve.wait_ge(x_ok, n + (x_base + 1))
                                dve.sem_inc(rel, 1)

                    if layer == 1 and last:
                        for i in range(KC // RING):
                            down(i, RING if i + 1 < KC // RING else RING - 2)
                    else:
                        with dve.Fori(0, KC // RING) as i:
                            down(i, RING)

                with dve.Fori(0, GROUPS) as g:
                    group(g, GROUP, turn0 + g * GROUP_TURNS, False)
                group(GROUPS, REST, turn0 + GROUPS * GROUP_TURNS, True)

            ffn(0, TURN_FFN0, KC)
            renorm(3, 3 * KC, None)

            ATT_STEPS = 3 * TB
            with dve.Fori(0, HEADS) as h:
                turn = TURN_ATT + h
                for s, (hi, lo, base) in enumerate(((Qh, Ql, 0), (Kh, Kl, 2))):
                    w_lo_of(turn, s)
                    for hf in range(2):
                        cs = slice(hf * HT, (hf + 1) * HT)
                        dve.wait_ge(mm, n_half(turn, s, hf))
                        dve.tensor_tensor(sc[:, 0, cs], ps[:, hf, :], rstd[:, cs], ALU.mult).then_inc(pj_t, 1)
                        dve.wait_ge(pj_hi, h * 4 + (base + hf + 1))
                        dve.tensor_tensor(lo[:, cs], sc[:, 0, cs], hi[:, cs].bitcast(F32),
                                          ALU.subtract).then_inc(qk_lo, 1)
                        dve.sem_inc(pj_ev, 1)
                w_lo_of(turn, 2)
                for hf in range(2):
                    cs = slice(hf * HT, (hf + 1) * HT)
                    dve.wait_ge(mm, n_half(turn, 2, hf))
                    dve.tensor_tensor(vT[:, cs], ps[:, hf, :], rstd[:, cs], ALU.mult).then_inc(pj_ev, 1)
                for hf in range(2):
                    dve.wait_ge(v_hi, h * 2 + (hf + 1))
                    dve.tensor_tensor(flat(Vl[:, 4 * hf:4 * hf + 4, :]), ps[:, 6 + hf, :],
                                      flat(Vh[:, 4 * hf:4 * hf + 4, :]).bitcast(F32), ALU.subtract).then_inc(v_lo, 1)
                dve.wait_ge(bias_ok, h + 4)
                g = 0
                for i in range(TB):
                    w = (i + 1) * P
                    b0 = (TB - 1 - i) * P
                    for c in range(2):
                        dve.wait_ge(s_mm, h * (2 * TB) + (2 * i + c + 1))
                        if c == 0 and i:
                            dve.wait_ge(tr_mm, h * 12 + g)
                        apart(dve)
                        dve.tensor_tensor_reduce(sc[:, c, 0:w], flat(ps[:, 2 + 2 * c:4 + 2 * c, :])[:, 0:w],
                                                 bias[:, b0:b0 + w], -QK_SCALE, 3e38, ALU.add, ALU.min,
                                                 negmax[:, c:c + 1]).then_inc(s_ev, 1)
                    dve.wait_ge(e_ok, h * (2 * TB) + (2 * i + 2))
                    dve.reciprocal(rrow, rowsum).then_inc(att_s, 1)
                    dve.wait_ge(att_s, h * ATT_STEPS + (3 * i + 1))
                    dve.tensor_tensor(rlam, rrow[:, 1:2], neg_lam, ALU.mult).then_inc(att_s, 1)
                    dve.wait_ge(att_s, h * ATT_STEPS + (3 * i + 2))
                    dve.tensor_scalar(sc[:, 1, 0:w], sc[:, 1, 0:w], rlam, None, ALU.mult).then_inc(att_s, 1)
                    dve.wait_ge(att_s, h * ATT_STEPS + (3 * i + 3))
                    dve.scalar_tensor_tensor(sc[:, 0, 0:w], sc[:, 0, 0:w], rrow[:, 0:1], sc[:, 1, 0:w],
                                             ALU.mult, ALU.add).then_inc(a_ok, 1)
                    for j0 in range(0, i + 1, 4):
                        nj = min(4, i + 1 - j0)
                        qs = slice((i % 2) * P, (i % 2 + 1) * P)
                        dve.wait_ge(at_hi, h * 12 + (g + 1))
                        dve.tensor_tensor(ATl[:, j0:j0 + nj, qs],
                                          ps[:, 6 + g % 2, 0:nj * P].rearrange("p (j q) -> p j q", q=P),
                                          ATh[:, j0:j0 + nj, qs].bitcast(F32), ALU.subtract).then_inc(tr_ev, 1)
                        g += 1
                w_lo_of(turn, 3)
                for hf in range(2):
                    cs = slice(hf * HT, (hf + 1) * HT)
                    dve.wait_ge(ostd_ok, h * 2 + (hf + 1))
                    dve.reciprocal(sc[:, 1, cs], sc[:, 1, cs]).then_inc(orec_ok, 1)
                for hf in range(2):
                    cs = slice(hf * HT, (hf + 1) * HT)
                    dve.wait_ge(orec_ok, h * 2 + (hf + 1))
                    dve.tensor_tensor(vT[:, cs], ps[:, hf, :], sc[:, 1, cs], ALU.mult).then_inc(pj_ev, 1)
                for hf in range(2):
                    cs = slice(hf * HT, (hf + 1) * HT)
                    dve.wait_ge(o_hi, h * 2 + (hf + 1))
                    dve.scalar_tensor_tensor(Ol[:, cs], vT[:, cs], sub_g, Oh[:, cs].bitcast(F32),
                                             ALU.mult, ALU.subtract).then_inc(o_lo, 1)
                for m in range(16):
                    n, hf = m // 2, m % 2
                    xs = xT[:, n, hf * HT:(hf + 1) * HT]
                    if m < 15:
                        dve.wait_ge(wo_mm, h * 15 + (m + 1))
                    else:
                        dve.wait_ge(mm, n_half(turn, 3, 1))
                    dve.tensor_tensor(xs, ps[:, 2 + m % 4, :], xs, ALU.add).then_inc(wo_ev, 1)
            renorm(4, 4 * KC, "ffn_norm_g", KC)
            ffn(1, TURN_FFN1, 2 * KC)

            recip(5)
            for hf in range(2):
                cs = slice(hf * HT, (hf + 1) * HT)
                for k in range(KC):
                    dve.scalar_tensor_tensor(xT[:, k, cs], xT[:, k, cs], col("final_norm_g", k), rstd[:, cs],
                                             ALU.mult, ALU.mult).then_inc(y_ok, 1)

        @block.tensor
        def _(pe):
            def transpose(dst, src, m=P):
                return pe.transpose(dst, src, ident[0:m, 0:m])

            pe.wait_ge(consts, 4)
            pe.wait_ge(vec_in, 16 * (len(VECS) + 5))
            transpose(ps[:, 6, 0:NVEC], vrow[0:NVEC, :], NVEC).then_inc(vec_t, 1)
            for s in range(2):
                transpose(ps[:, 7, s * P:s * P + DWR], dwrow[:, s, :], DWR).then_inc(vec_t, 1)
            for t in range(TB):
                pe.wait_ge(x_in[t], 16)
                if t == 3:
                    pe.wait_ge(vec_ev, 3)
                if t >= 4:
                    pe.wait_ge(xt_ev, t - 3)
                for k in range(KC):
                    ins = transpose(ps[:, 2 * (t % 4) + k // 4, (k % 4) * P:(k % 4 + 1) * P],
                                    xrow[:, t, k * P:(k + 1) * P])
                ins.then_inc(xt_mm, 1)

            def product(dst, lh, ll, rh, rl, start, stop):
                pe.matmul(dst, ll, rh, start=start, stop=False)
                pe.matmul(dst, lh, rl, start=False, stop=False)
                return pe.matmul(dst, lh, rh, start=False, stop=stop)

            def dense(turn, s, src_h, src_l, chunks, rel_off=0, ready=None, bank=None):
                pe.wait_ge(w_lo, n_block(turn, s))
                if bank is None:
                    pe.wait_ge(rel, n_rel(turn, s) - rel_off)
                for hf in range(2):
                    cs = slice(hf * HT, (hf + 1) * HT)
                    dst = ps[:, (2 * s if bank is None else bank) + hf, :]
                    for k in range(chunks):
                        if ready is not None:
                            ready(hf, k)
                        ins = product(dst, Wh[s][:, k, :], Wl[s][:, k, :], src_h[:, k, cs], src_l[:, k, cs],
                                      k == 0, k == chunks - 1)
                    ins.then_inc(mm, 1)

            def variance(n):
                pe.wait_ge(acc_ok, (KC + 1) * (n + 1))
                for hf in range(2):
                    pe.matmul(ps[:, var_bank[n] + hf, :], ones[:, :], acc[:, hf * HT:(hf + 1) * HT],
                              start=True, stop=True).then_inc(var_mm, 1)

            def s_ready(base):
                def ready(hf, k):
                    if hf == 0:
                        pe.wait_ge(s_lo, base + k + 1)
                return ready

            pe.wait_ge(xt_ev, TB)
            dense(0, 0, Sh, Sl, KC, ready=s_ready(0))
            dense(0, 1, Sh, Sl, KC)
            variance(0)
            dense(0, 2, Sh, Sl, KC)
            pe.wait_ge(std_ok, 2)
            dense(0, 3, Sh, Sl, KC)
            with pe.Fori(1, 2 * KC // RING) as i:
                for s in range(RING):
                    dense(i, s, Sh, Sl, KC)

            pe.wait_ge(rel, TURN_PW2 * RING + RING)
            for k in range(KC):
                pe.wait_ge(cv_ok, k + 1)
                for hf in range(2):
                    ins = pe.matmul(ps[:, hf, :], ones[:, :], cv[:, k, hf * HT:(hf + 1) * HT],
                                    start=k == 0, stop=k == KC - 1)
                    if k == KC - 1:
                        ins.then_inc(mean_mm, 1)
            variance(1)

            dense(TURN_PW2, 0, Sh, Sl, KC, ready=s_ready(KC))
            for s in range(1, RING):
                dense(TURN_PW2, s, Sh, Sl, KC)
            with pe.Fori(1, KC // RING) as i:
                for s in range(RING):
                    dense(TURN_PW2 + i, s, Sh, Sl, KC)

            def ffn(layer, turn0, n, s_base, off):
                def up_turn(turn, first=False):
                    for s in range(RING):
                        if first and s == 2:
                            variance(n)
                        if first and s == 3:
                            pe.wait_ge(std_ok, 2 * n + 2)
                        dense(turn, s, Sh, Sl, KC, off, s_ready(s_base) if first and s == 0 else None)

                def down(g, size, turn):
                    base = 2 * FC * layer + 1

                    def ready(hf, k):
                        pe.wait_ge(hid_lo, g * (2 * GROUP) + (base + 2 * k + hf))
                    with pe.Fori(0, KC // RING) as i:
                        for s in range(RING):
                            dense(turn + i, s, Gh, Gl, size, off, ready if s == 0 else None)

                up_turn(turn0, True)
                with pe.Fori(1, GROUP // 2) as i:
                    up_turn(turn0 + i)
                down(0, GROUP, turn0 + GROUP // 2)
                with pe.Fori(1, GROUPS) as g:
                    with pe.Fori(0, GROUP // 2) as i:
                        up_turn(turn0 + g * GROUP_TURNS + i)
                    down(g, GROUP, turn0 + g * GROUP_TURNS + GROUP // 2)
                turn = turn0 + GROUPS * GROUP_TURNS
                with pe.Fori(0, REST // 2) as i:
                    up_turn(turn + i)
                down(GROUPS, REST, turn + REST // 2)

            ffn(0, TURN_FFN0, 2, 2 * KC, 0)

            pe.wait_ge(rel, TURN_ATT * RING + RING)
            variance(3)

            def head(h, first):
                turn = TURN_ATT + h
                for s in range(3):
                    pe.wait_ge(w_lo, n_block(turn, s))
                    for hf in range(2):
                        cs = slice(hf * HT, (hf + 1) * HT)
                        pe.wait_ge(pj_ev, h * 8 + (2 * s + hf + 1))
                        for k in range(KC):
                            if first and s == 0 and hf == 0:
                                pe.wait_ge(s_lo, 3 * KC + k + 1)
                            ins = product(ps[:, hf, :], Wh[s][:, k, :], Wl[s][:, k, :], Sh[:, k, cs], Sl[:, k, cs],
                                          k == 0, k == KC - 1)
                        ins.then_inc(mm, 1)
                pe.wait_ge(tr_ev, h * 12 + 2)
                for hf in range(2):
                    pe.wait_ge(pj_ev, h * 8 + (4 + hf + 3))
                    for j in range(4):
                        ins = transpose(ps[:, 6 + hf, j * P:(j + 1) * P], vT[:, (4 * hf + j) * P:(4 * hf + j + 1) * P])
                    ins.then_inc(vt_mm, 1)
                pe.wait_ge(qk_lo, h * 4 + 4)
                pe.wait_ge(wo_ev, h * 16 + 4)

                def scores(i):
                    qs = slice(i * P, (i + 1) * P)
                    for c in range(2):
                        cp = slice(c * HD, (c + 1) * HD)
                        pe.wait_ge(s_ev, h * (2 * TB) + (2 * i + c + 1))
                        for n0 in range(0, (i + 1) * P, HT):
                            n1 = min((i + 1) * P, n0 + HT)
                            ins = product(ps[:, 2 + 2 * c + n0 // HT, 0:n1 - n0], Qh[cp, qs], Ql[cp, qs],
                                          Kh[cp, n0:n1], Kl[cp, n0:n1], True, True)
                        ins.then_inc(s_mm, 1)

                g = 0
                scores(0)
                for i in range(TB):
                    if i + 1 < TB:
                        scores(i + 1)
                    pe.wait_ge(a_ok, h * TB + (i + 1))
                    if i == 0:
                        pe.wait_ge(v_lo, h * 2 + 2)
                    for j0 in range(0, i + 1, 4):
                        pe.wait_ge(tr_ev, h * 12 + (g + 1))
                        for j in range(j0, min(j0 + 4, i + 1)):
                            ins = transpose(ps[:, 6 + g % 2, (j - j0) * P:(j - j0 + 1) * P], sc[:, 0, j * P:(j + 1) * P])
                        ins.then_inc(tr_mm, 1)
                        g += 1
                    if i % 2:
                        q0 = (i // 2 % 2) * 2 * P
                        pe.wait_ge(tr_ev, h * 12 + (g + 2))
                        pe.wait_ge(pj_ev, h * 8 + (6 + i // 4 + 1))
                        for j in range(i + 1):
                            c0 = P if j == i else 0
                            ins = product(ps[:, i // 4, q0 + c0:q0 + 2 * P], Vh[:, j, :], Vl[:, j, :],
                                          ATh[:, j, c0:2 * P], ATl[:, j, c0:2 * P], j == 0, j == i)
                        ins.then_inc(pv_mm, 1)
                for hf in range(2):
                    pe.wait_ge(osq_ok, h * 2 + (hf + 1))
                    pe.matmul(ps[:, 4 + hf, :], ones[:, :], vT[:, hf * HT:(hf + 1) * HT], start=True,
                              stop=True).then_inc(ov_mm, 1)
                pe.wait_ge(w_lo, n_block(turn, 3))
                pe.wait_ge(o_lo, h * 2 + 2)
                for m in range(16):
                    n, hf = m // 2, m % 2
                    cs = slice(hf * HT, (hf + 1) * HT)
                    pe.wait_ge(wo_ev, h * 16 + (m + 1))
                    ins = product(ps[:, 2 + m % 4, :], Wh[3][:, n, :], Wl[3][:, n, :], Oh[:, cs], Ol[:, cs], True, True)
                    if m < 15:
                        ins.then_inc(wo_mm, 1)
                    else:
                        ins.then_inc(mm, 2)

            head(0, True)
            with pe.Fori(1, HEADS) as h:
                head(h, False)
            pe.wait_ge(wo_ev, HEADS * 16 + 4)
            ffn(1, TURN_FFN1, 4, 4 * KC, HEADS * RING)

            pe.wait_ge(rel, (TURNS - HEADS) * RING + RING)
            variance(5)
            for t in range(TB):
                pe.wait_ge(y_ok, KC * (t // 4 + 1))
                if t == 3:
                    pe.wait_ge(std_ok, 12)
                if t >= 4:
                    pe.wait_ge(yt_ev, t - 3)
                for k in range(KC):
                    ins = transpose(ps[:, 2 * (t % 4) + k // 4, (k % 4) * P:(k % 4 + 1) * P],
                                    xT[:, k, t * P:(t + 1) * P])
                ins.then_inc(yt_mm, 1)


var_bank = {0: 6, 1: 2, 2: 6, 3: 6, 4: 6, 5: 6}

_INS = ["x", "conv_norm_g", "pw1_w", "pw1_b", "dw_w", "dw_b", "conv_ln_g", "conv_ln_b", "pw2_w", "pw2_b", "kv_norm_g",
        "w_k", "w_v", "attn_norm_g", "w_q", "lambda_q1", "lambda_k1", "lambda_q2", "lambda_k2", "subln_g", "w_o",
        "ffn_norm_g", "ffn_w1", "ffn_w3", "ffn_w2", "final_norm_g"]


def kernel(**inputs):
    import numpy as _np
    import concourse.bacc as _bacc
    from concourse import mybir as _mybir
    from concourse.bass_utils import run_bass_kernel_spmd as _run

    nc = _bacc.Bacc("TRN2", target_bir_lowering=False, num_devices=1)
    arrays, args = {}, {}
    for name in _INS:
        v = _np.ascontiguousarray(inputs[name])
        arrays[f"in_{name}_dram"] = v
        args[name] = nc.dram_tensor(f"in_{name}_dram", v.shape, _mybir.dt.from_np(v.dtype), kind="ExternalInput").ap()
    out = nc.dram_tensor("out_0_dram", (1, T, D), F32, kind="ExternalOutput").ap()
    trunk(nc, args, out)
    r = _run(nc, [arrays], core_ids=[0])
    return r.results[0]["out_0_dram"]
```

```python
import math
from contextlib import ExitStack

import concourse.bass as bass
from concourse import mybir

F32 = mybir.dt.float32
F32R = mybir.dt.float32r
F16 = mybir.dt.float16
ALU = mybir.AluOpType
ACT = mybir.ActivationFunctionType
AX_X = mybir.AxisListType.X

P = 128
D = 1024
T = 1024
HT = 512
KC = D // P
TB = T // P
F = 2816
FC = F // P
CW = 31
PAD = CW - 1
HEADS = 8
HD = 64
EPS = 1e-6
LAMBDA_INIT = 0.8 - 0.6 * math.exp(-0.3)
QK_SCALE = HD ** -0.5
Q_SHIFT = 2.0 ** -9
MASKED = -65504.0
ACT_TAPS = 10
DVE_TAPS = CW - ACT_TAPS

RING = 4
GROUP = 6
GROUPS = FC // GROUP
REST = FC - GROUP * GROUPS
GROUP_TURNS = 2 * GROUP // RING + KC // RING
REST_TURNS = 2 * REST // RING + KC // RING
FFN_TURNS = GROUPS * GROUP_TURNS + REST_TURNS
TURN_PW1 = 0
TURN_PW2 = TURN_PW1 + 2 * KC // RING
TURN_FFN0 = TURN_PW2 + KC // RING
TURN_ATT = TURN_FFN0 + FFN_TURNS
TURN_FFN1 = TURN_ATT + HEADS
TURNS = TURN_FFN1 + FFN_TURNS

VECS = {}
for _name, _rows in (("conv_norm_g", KC), ("pw1_b", 2 * KC), ("dw_b", KC), ("conv_ln_g", KC), ("conv_ln_b", KC),
                     ("pw2_b", KC), ("ffn_norm_g", 2 * KC), ("kv_norm_g", KC), ("attn_norm_g", KC),
                     ("final_norm_g", KC), ("subln_g", 1)):
    VECS[_name] = (sum(r for _, r in VECS.values()), _rows)
NVEC = sum(r for _, r in VECS.values())
DWR = CW * KC // 2

KB = 1024
X_AT = 0
S_AT = 32 * KB
G_AT = S_AT + 64 * KB
RAW_AT = G_AT + 48 * KB
W_AT = RAW_AT + 8 * KB
RSTD_AT = W_AT + 32 * KB
R_AT = RSTD_AT + 4 * KB
SMALL_AT = R_AT + 18 * KB


def trunk(nc, a, out):
    with ExitStack() as ctx:
        base = -(-nc.sbuf_base // 64) * 64

        def at(name, shape, dt, offset):
            return nc.alloc_sbuf_tensor_at(name, shape, dt, offset=base + offset)

        def sem(name):
            return ctx.enter_context(nc.semaphore(name))

        xT = at("xT", [P, KC, T], F32, X_AT)
        Sh = at("Sh", [P, KC, T], F32R, S_AT)
        Sl = at("Sl", [P, KC, T], F32R, S_AT + 32 * KB)
        yout = at("yout", [P, TB, D], F32, S_AT)
        Gh = at("Gh", [P, GROUP, T], F32R, G_AT)
        Gl = at("Gl", [P, GROUP, T], F32R, G_AT + 24 * KB)
        xrow = at("xrow", [P, TB, D], F32, G_AT)
        vrow = at("vrow", [P, P], F32, G_AT + 32 * KB)
        dwrow = at("dwrow", [DWR, 2, P], F32, G_AT + 33 * KB)
        lamv = at("lamv", [P, 4, HD], F32, G_AT + 34 * KB)
        cv = at("cv", [P, KC, T], F32, G_AT)
        up = at("up", [P, 2, PAD + T + 2], F32, G_AT + 32 * KB)
        cacc = at("cacc", [P, T], F32, G_AT + 41 * KB)
        prod = at("prod", [P, T], F32, R_AT + 4 * KB)
        ATh = at("ATh", [P, TB, 2 * P], F32R, G_AT)
        ATl = at("ATl", [P, TB, 2 * P], F32R, G_AT + 8 * KB)
        Qh = at("Qh", [P, T], F32R, G_AT + 16 * KB)
        Ql = at("Ql", [P, T], F32R, G_AT + 20 * KB)
        Kh = at("Kh", [P, T], F32R, G_AT + 24 * KB)
        Kl = at("Kl", [P, T], F32R, G_AT + 28 * KB)
        Vh = at("Vh", [P, TB, P], F32R, G_AT + 32 * KB)
        Vl = at("Vl", [P, TB, P], F32R, G_AT + 36 * KB)
        Oh = at("Oh", [P, T], F32R, G_AT + 40 * KB)
        Ol = at("Ol", [P, T], F32R, G_AT + 44 * KB)
        raw = [at(f"raw{r}", [P, KC, P], F32, RAW_AT + r * 4 * KB) for r in range(2)]
        Wh = [at(f"Wh{r}", [P, KC, P], F32R, W_AT + r * 8 * KB) for r in range(RING)]
        Wl = [at(f"Wl{r}", [P, KC, P], F32R, W_AT + r * 8 * KB + 4 * KB) for r in range(RING)]
        rstd = at("rstd", [P, T], F32, RSTD_AT)
        acc = at("acc", [P, T], F32, R_AT)
        sq = at("sq", [P, T], F32, R_AT + 4 * KB)
        tmp = at("tmp", [P, 2, 2, HT], F32, R_AT + 8 * KB)
        mu = at("mu", [P, T], F32, R_AT + 8 * KB)
        vS = at("vS", [P, T], F32, R_AT)
        ob, rb = vS[:, 0:HT], vS[:, HT:T]
        bias = at("bias", [P, T], F16, R_AT + 4 * KB)
        sc0 = at("sc0", [P, 2, T], F32, R_AT + 6 * KB)
        sc1 = at("sc1", [P, T], F32, R_AT + 14 * KB)
        qS = at("qS", [P, T], F32, W_AT + 16 * KB)
        kS = at("kS", [P, T], F32, W_AT + 20 * KB)
        ident = at("ident", [P, P], F32, SMALL_AT)
        ones = at("ones", [P, P], F32, SMALL_AT + 512)
        vec = at("vec", [P, NVEC], F32, SMALL_AT + 1024)
        dw = at("dw", [P, 2 * DWR], F32, R_AT + 16 * KB)
        small = at("small", [P, 32], F32, SMALL_AT + 1024 + 416)
        eps = small[:, 0:1]
        neg_lam = small[:, 1:2]
        sub_g = small[:, 2:3]
        lsum = small[:, 4:6]
        lexp = small[:, 6:8]
        negmax = small[:, 8:12]
        rowsum = small[:, 12:16]
        rrow = small[:, 16:18]
        rlam = small[:, 18:19]
        lpair = at("lpair", [P, 2, HD], F32, G_AT + 35 * KB)
        ps = nc.alloc_psum_tensor("ps", [P, 8, HT], F32)

        def col(name, k=0):
            return vec[:, bass.ds(VECS[name][0] + k, 1)]

        consts = sem("consts")
        vec_in = sem("vec_in")
        x_in = [sem(f"x_in{t}") for t in range(TB)]
        vec_t = sem("vec_t")
        vec_ev = sem("vec_ev")
        xt_mm = sem("xt_mm")
        xt_ev = sem("xt_ev")
        lam_s = sem("lam_s")
        lam_e = sem("lam_e")
        raw_in = [sem(f"raw_in{r}") for r in range(2)]
        raw_ok = sem("raw_ok")
        w_hi = sem("w_hi")
        w_lo = sem("w_lo")
        mm = sem("mm")
        rel = sem("rel")
        s_hi = sem("s_hi")
        s_lo = sem("s_lo")
        sq_ok = sem("sq_ok")
        acc_ok = sem("acc_ok")
        var_mm = sem("var_mm")
        std_ok = sem("std_ok")
        rstd_ok = sem("rstd_ok")
        gate_t = sem("gate_t")
        gate_s = sem("gate_s")
        val_t = sem("val_t")
        glu_ok = sem("glu_ok")
        prod_ok = sem("prod_ok")
        tap_ok = sem("tap_ok")
        conv_s = sem("conv_s")
        cv_ok = sem("cv_ok")
        mean_mm = sem("mean_mm")
        mu_ok = sem("mu_ok")
        xc_ok = sem("xc_ok")
        ln_t = sem("ln_t")
        ln_y = sem("ln_y")
        x_ok = sem("x_ok")
        t1_ok = sem("t1_ok")
        silu_ok = sem("silu_ok")
        t3_ok = sem("t3_ok")
        hid_t = sem("hid_t")
        hid_hi = sem("hid_hi")
        hid_lo = sem("hid_lo")
        bias_ok = sem("bias_ok")
        pj_mm = sem("pj_mm")
        pj_ev = sem("pj_ev")
        qk_hi = sem("qk_hi")
        qk_lo = sem("qk_lo")
        s_mm = sem("s_mm")
        s_ev = sem("s_ev")
        e_ok = sem("e_ok")
        att_s = sem("att_s")
        a_ok = sem("a_ok")
        tr_mm = sem("tr_mm")
        tr_hi = sem("tr_hi")
        tr_ev = sem("tr_ev")
        pv_mm = sem("pv_mm")
        osq_ok = sem("osq_ok")
        ov_mm = sem("ov_mm")
        ostd_ok = sem("ostd_ok")
        orec_ok = sem("orec_ok")
        o_ev = sem("o_ev")
        o_hi = sem("o_hi")
        o_lo = sem("o_lo")
        wo_mm = sem("wo_mm")
        wo_ev = sem("wo_ev")
        y_ok = sem("y_ok")
        yt_mm = sem("yt_mm")
        yt_ev = sem("yt_ev")
        went_on = sem("went_on")
        stored = sem("stored")

        block = ctx.enter_context(nc.Block())

        def apart(eng):
            eng.sem_inc(went_on, 1)

        def flat(ap):
            return ap.rearrange("p a b -> p (a b)")

        def n_block(turn, s):
            return turn * RING + s + 1

        def n_half(turn, s, hf, off=0):
            return turn * (2 * RING) + (2 * s + hf + 1 - 2 * off)

        def n_rel(turn, s):
            return turn * RING + s + 1

        ATT0 = TURN_ATT * RING
        Q_R, K_R, V_R, O_R = range(4)
        SLOT = {Q_R: 0, K_R: 1, V_R: 0, O_R: 3}

        def att_block(h, r):
            return h * 4 + (ATT0 + 3 + r)

        def att_stage(r):
            return (ATT0 + 3 + r) % 2

        def att_landed(h, r):
            return h * 32 + 16 * ((ATT0 + 3 + r) // 2 + 1)

        TR = 14
        TR_AT = [2 + sum(1 + j // 4 for j in range(i)) for i in range(TB)]

        def groups(i):
            return range(0, i + 1, 4)

        BESIDE = [("w", "w", "w", ""), ("ppp", "ppw", "pppw", ""), ("ppp", "pp", "pwppw", ""),
                  ("ppw", "ppp", "wppp", ""), ("ppw", "pp", "wpp", "pp"), ("pp", "ppw", "pp", "w"),
                  ("pp", "p", "p", "p"), ("pp", "", "wwp", "ppw")]
        EARLY = BESIDE[TB - 1][2].count("w") + BESIDE[TB - 1][3].count("w")

        def beside(i, part, on_p, on_w):
            done = "".join("".join(b) for b in BESIDE[:i]) + "".join(BESIDE[i][:part])
            p, w = done.count("p"), done.count("w") + EARLY
            for c in BESIDE[i][part]:
                if c == "p":
                    on_p(p // KC, p % KC)
                    p += 1
                else:
                    on_w(-1 if w < 2 * KC else 0, w % (2 * KC))
                    w += 1

        def units_before(i, part=0):
            return EARLY + ("".join("".join(b) for b in BESIDE[:i]) + "".join(BESIDE[i][:part])).count("w")

        w1, w3, w2 = a["ffn_w1"], a["ffn_w3"], a["ffn_w2"]

        @block.sync
        def _(sp):
            for n, (name, (at0, rows)) in enumerate(VECS.items()):
                src = a[name]
                flat_src = src.rearrange("a (r p) -> (a r) p", p=P) if len(src.shape) == 2 else \
                    src.rearrange("(r p) -> r p", p=P)
                sp.dma_start(vrow[at0:at0 + rows, :], flat_src).then_inc(vec_in, 16)
            sp.dma_start(dwrow[:, :, :], a["dw_w"][0].rearrange("j (c p) -> (j c) p", p=P)
                         .rearrange("(s q) p -> q s p", s=2)).then_inc(vec_in, 16)
            for n, name in enumerate(("lambda_q1", "lambda_k1", "lambda_q2", "lambda_k2")):
                sp.dma_start(lamv[:, n, :], a[name].broadcast_to([P, HD])).then_inc(vec_in, 16)
            xin = a["x"][0].rearrange("(t p) d -> t p d", p=P)
            for t in range(2):
                sp.dma_start(xrow[:, t, :], xin[t]).then_inc(x_in[t], 16)

            def load(turn, s, src, first=False):
                if not first:
                    sp.wait_ge(w_lo, turn * RING + (s - 1))
                sp.dma_start(raw[s % 2][:, 0:src.shape[1], :] if len(src.shape) == 3 else flat(raw[s % 2]),
                             src).then_inc(raw_in[s % 2], 16)

            pw1 = a["pw1_w"][0].rearrange("(k p) n -> p k n", p=P)
            pw2 = a["pw2_w"][0].rearrange("(k p) n -> p k n", p=P)

            def pw1_turn(i, first=False):
                for s in range(RING):
                    c0 = (2 * i + s // 2) * P + (s % 2) * D
                    load(TURN_PW1 + i, s, pw1[:, :, bass.ds(c0, P)], first and s < 2)
                    if first and s == 1:
                        for t in range(2, TB):
                            sp.dma_start(xrow[:, t, :], xin[t]).then_inc(x_in[t], 16)

            pw1_turn(0, True)
            with sp.Fori(1, 2 * KC // RING) as i:
                pw1_turn(i)
            with sp.Fori(0, KC // RING) as i:
                for s in range(RING):
                    load(TURN_PW2 + i, s, pw2[:, :, bass.ds((RING * i + s) * P, P)])

            def ffn(layer, turn0):
                u1 = w1[layer].rearrange("(k p) n -> p k n", p=P)
                u3 = w3[layer].rearrange("(k p) n -> p k n", p=P)
                u2 = w2[layer].rearrange("(k p) n -> p k n", p=P)

                def group(g, size, turn):
                    with sp.Fori(0, size // 2) as i:
                        for s in range(RING):
                            c0 = (g * GROUP + 2 * i + s // 2) * P
                            load(turn + i, s, (u3 if s % 2 else u1)[:, :, bass.ds(c0, P)])
                    with sp.Fori(0, KC // RING) as i:
                        for s in range(RING):
                            load(turn + size // 2 + i, s,
                                 u2[:, bass.ds(g * GROUP, size), bass.ds((RING * i + s) * P, P)])

                with sp.Fori(0, GROUPS) as g:
                    group(g, GROUP, turn0 + g * GROUP_TURNS)
                group(GROUPS, REST, turn0 + GROUPS * GROUP_TURNS)

            ffn(0, TURN_FFN0)
            wq = a["w_q"][0].rearrange("(k p) n -> p k n", p=P)
            wk = a["w_k"].rearrange("(k p) n -> p k n", p=P)
            wv = a["w_v"].rearrange("(k p) n -> p k n", p=P)

            def att_load(h, r, src):
                st = raw[att_stage(r)]
                sp.wait_ge(w_lo, att_block(h, r) - 1)
                sp.dma_start(st[:, :, :] if len(src.shape) == 3 else flat(st), src).then_inc(raw_in[att_stage(r)], 16)

            def qkv_cols(w, h):
                return w[:, :, bass.ds(h * P, P)]

            wo = a["w_o"][0]
            for b, w in enumerate((wq, wk, wv)):
                att_load(0, b - 3, qkv_cols(w, 0))

            def head_blocks(h):
                for r, w in ((Q_R, wq), (K_R, wk), (V_R, wv)):
                    att_load(h, r, qkv_cols(w, h + 1))
                att_load(h, O_R, wo[bass.ds(h * P, P), :])

            with sp.Fori(0, HEADS - 1) as h:
                head_blocks(h)
            att_load(HEADS - 1, 0, wo[(HEADS - 1) * P:HEADS * P, :])
            ffn(1, TURN_FFN1)

            for t in range(TB):
                sp.wait_ge(yt_ev, t + 1)
                sp.dma_start(out[0, t * P:(t + 1) * P, :], yout[:, t, :]).then_inc(stored, 16)
            sp.wait_ge(stored, 16 * TB)

        @block.gpsimd
        def _(pool):
            pool.memset(ident[:, :], 0.0).then_inc(consts, 1)
            pool.memset(ones[:, :], 1.0).then_inc(consts, 1)
            pool.memset(eps, EPS).then_inc(consts, 1)
            pool.wait_ge(consts, 1)
            pool.affine_select(out=ident[:, :], in_=ident[:, :], compare_op=ALU.not_equal, fill=1.0, base=0,
                               pattern=[[-1, P]], channel_multiplier=1).then_inc(consts, 1)

            def passed(turn, s, gain=None):
                pool.wait_ge(raw_in[s % 2], turn * 32 + 16 * (s // 2 + 1))
                if gain is None:
                    pool.sem_inc(raw_ok, 1)
                else:
                    at0 = VECS[gain][0]
                    g = vec[:, at0:at0 + KC].unsqueeze(2).to_broadcast([P, KC, P])
                    r = raw[s % 2][:, :, :]
                    pool.tensor_tensor(r, r, g, ALU.mult).then_inc(raw_ok, 1)
                    pool.wait_ge(raw_ok, n_block(turn, s))

            def pass_turns(turn0, turns):
                with pool.Fori(0, turns) as i:
                    for s in range(RING):
                        passed(turn0 + i, s)

            def sum_squares(n):
                if n:
                    pool.wait_ge(var_mm, 2 * n)
                pool.memset(acc[:, :], 0.0).then_inc(acc_ok, 1)
                with pool.Fori(0, KC) as k:
                    pool.wait_ge(sq_ok, k + (KC * n + 1))
                    pool.wait_ge(acc_ok, k + ((KC + 1) * n + 1))
                    pool.tensor_tensor(acc[:, :], acc[:, :], sq[:, :], ALU.add).then_inc(acc_ok, 1)
                pool.wait_ge(acc_ok, (KC + 1) * (n + 1))

            passed(TURN_PW1, 0)
            passed(TURN_PW1, 1)
            sum_squares(0)
            passed(TURN_PW1, 2)
            passed(TURN_PW1, 3)

            def conv_taps(n):
                for j in range(1, ACT_TAPS):
                    pool.wait_ge(prod_ok, n * ACT_TAPS + (j + 1))
                    if j > 1:
                        pool.wait_ge(tap_ok, n * (ACT_TAPS - 1) + (j - 1))
                    pool.tensor_tensor(cacc[:, :], cacc[:, :], prod[:, :], ALU.add).then_inc(tap_ok, 1)

            with pool.Fori(0, KC // 2 - 1) as i:
                passed(i + 1, 0)
                passed(i + 1, 1)
                conv_taps(2 * i)
                passed(i + 1, 2)
                passed(i + 1, 3)
                conv_taps(2 * i + 1)
            passed(TURN_PW2, 0)
            passed(TURN_PW2, 1)
            conv_taps(KC - 2)
            conv_taps(KC - 1)
            sum_squares(1)
            passed(TURN_PW2, 2)
            passed(TURN_PW2, 3)
            pass_turns(TURN_PW2 + 1, 1)
            passed(TURN_FFN0, 0)
            passed(TURN_FFN0, 1)
            sum_squares(2)
            passed(TURN_FFN0, 2)
            passed(TURN_FFN0, 3)
            pass_turns(TURN_FFN0 + 1, FFN_TURNS - 1)

            def att_passed(h, r, gain=None):
                pool.wait_ge(raw_in[att_stage(r)], att_landed(h, r))
                if gain is None:
                    pool.sem_inc(raw_ok, 1)
                else:
                    at0 = VECS[gain][0]
                    g = vec[:, at0:at0 + KC].unsqueeze(2).to_broadcast([P, KC, P])
                    rw = raw[att_stage(r)][:, :, :]
                    pool.tensor_tensor(rw, rw, g, ALU.mult).then_inc(raw_ok, 1)
                    pool.wait_ge(raw_ok, att_block(h, r) + 1)

            att_passed(0, -3, "attn_norm_g")
            att_passed(0, -2, "kv_norm_g")
            sum_squares(3)
            bt = bias[:, :]
            pool.iota(sc1[:, :], pattern=[[1, T]], base=-(T - P), channel_multiplier=-1,
                      allow_small_or_imprecise_dtypes=True).then_inc(bias_ok, 1)
            pool.wait_ge(bias_ok, 1)
            pool.tensor_scalar(bt, sc1[:, :], Q_SHIFT / QK_SCALE, 0.0, ALU.mult, ALU.add).then_inc(bias_ok, 1)

            def head_bias(h):
                pool.wait_ge(s_ev, h * (2 * TB) + 2)
                apart(pool)
                pool.wait_ge(bias_ok, 2 * h + 2)
                apart(pool)
                pool.tensor_scalar(bt, bt, 0.5, 0.0, ALU.mult, ALU.add).then_inc(bias_ok, 1)
                pool.wait_ge(bias_ok, 2 * h + 3)
                apart(pool)
                pool.affine_select(out=bias[:, T - P:T], in_=bias[:, T - P:T], compare_op=ALU.is_ge, fill=MASKED,
                                   base=0, pattern=[[-1, P]], channel_multiplier=1).then_inc(bias_ok, 1)

            att_passed(0, -1, "kv_norm_g")

            def head_pool(h):
                att_passed(h, Q_R, "attn_norm_g")
                head_bias(h)
                att_passed(h, K_R, "kv_norm_g")
                att_passed(h, V_R, "kv_norm_g")
                att_passed(h, O_R)

            head_bias(0)
            att_passed(0, Q_R, "attn_norm_g")
            att_passed(0, K_R, "kv_norm_g")
            att_passed(0, V_R, "kv_norm_g")
            att_passed(0, O_R)
            with pool.Fori(1, HEADS - 1) as h:
                head_pool(h)
            head_bias(HEADS - 1)
            att_passed(HEADS - 1, 0)
            passed(TURN_FFN1, 0)
            passed(TURN_FFN1, 1)
            pool.wait_ge(wo_ev, HEADS * 16 + 1)
            sum_squares(4)
            passed(TURN_FFN1, 2)
            passed(TURN_FFN1, 3)
            pass_turns(TURN_FFN1 + 1, FFN_TURNS - 1)
            sum_squares(5)

        @block.scalar
        def _(act):
            def squares(n, k, src):
                act.wait_ge(acc_ok, k + ((KC + 1) * n + 1))
                apart(act)
                act.activation(sq[:, :], src, ACT.Square).then_inc(sq_ok, 1)

            def root(n):
                for hf in range(2):
                    act.wait_ge(var_mm, 2 * n + hf + 1)
                    act.activation(rstd[:, hf * HT:(hf + 1) * HT], ps[:, var_bank[n] + hf, :], ACT.Sqrt, bias=eps,
                                   scale=1.0 / D).then_inc(std_ok, 1)

            def renorm(n, x_base, hi_base, gain, gain_at=0):
                with act.Fori(0, KC) as k:
                    if x_base is not None:
                        act.wait_ge(x_ok, k + (x_base + 1))
                        apart(act)
                    act.activation(Sh[:, k, :], xT[:, k, :], ACT.Copy,
                                   scale=1.0 if gain is None else col(gain, gain_at + k)).then_inc(s_hi, 1)
                    squares(n, k, xT[:, k, :])
                root(n)

            for t in range(TB):
                act.wait_ge(xt_mm, t + 1)
                act.activation(xT[:, :, t * P:(t + 1) * P],
                               ps[:, 2 * (t % 4):2 * (t % 4) + 2, :].rearrange("p b (c q) -> p (b c) q", q=P),
                               ACT.Copy).then_inc(xt_ev, 1)
                if t == 0:
                    act.wait_ge(lam_s, 2)
                    act.activation(lexp, lsum, ACT.Exp).then_inc(lam_e, 1)
            act.wait_ge(raw_ok, 1)
            act.activation(flat(Wh[0]), flat(raw[0]), ACT.Copy).then_inc(w_hi, 1)
            act.wait_ge(raw_ok, 2)
            act.activation(flat(Wh[1]), flat(raw[1]), ACT.Copy).then_inc(w_hi, 1)
            act.wait_ge(vec_ev, 3)
            act.wait_ge(xt_ev, TB)
            renorm(0, None, 0, "conv_norm_g")

            def pw1_pair(turn, n, cc, next_turn, first=False):
                for s in (0, 1):
                    b = 2 * cc + s + 2
                    if first and b < RING:
                        act.wait_ge(raw_ok, b + 1)
                        act.activation(flat(Wh[b]), flat(raw[b % 2]), ACT.Copy).then_inc(w_hi, 1)
                    else:
                        w_split(turn, 2 * cc + s)
                for hf in range(2):
                    act.wait_ge(gate_t, n * 2 + (hf + 1))
                    apart(act)
                    act.activation(tmp[:, hf, 0, :], tmp[:, hf, 0, :], ACT.Sigmoid,
                                   bias=col("pw1_b", KC + n)).then_inc(gate_s, 1)
                act.wait_ge(glu_ok, n * 2 + 3)
                for j in range(ACT_TAPS):
                    if j == 0:
                        if not (first and cc == 0):
                            act.wait_ge(cv_ok, n)
                        dst = cacc
                    else:
                        if j == 1 and not (first and cc == 0):
                            act.wait_ge(tap_ok, n * (ACT_TAPS - 1))
                        if j > 1:
                            act.wait_ge(tap_ok, n * (ACT_TAPS - 1) + (j - 1))
                        dst = prod
                    act.activation(dst[:, :], up[:, cc, j:j + T], ACT.Copy,
                                   scale=dw[:, bass.ds(j * KC + n, 1)]).then_inc(prod_ok, 1)

            def w_split(turn, s, off=0):
                t2, s2 = turn + (s + 2) // RING, (s + 2) % RING
                act.wait_ge(raw_ok, n_block(t2, s2))
                act.wait_ge(mm, n_half(t2, s2, 1, off) - 2 * RING)
                act.activation(flat(Wh[s2]), flat(raw[s2 % 2]), ACT.Copy).then_inc(w_hi, 1)

            for cc in range(2):
                pw1_pair(0, cc, cc, 1, True)
            with act.Fori(1, KC // 2) as i:
                for cc in range(2):
                    pw1_pair(i, 2 * i + cc, cc, i + 1)

            for hf in range(2):
                act.wait_ge(mean_mm, hf + 1)
                act.activation(mu[:, hf * HT:(hf + 1) * HT], ps[:, hf, :], ACT.Copy, scale=1.0 / D).then_inc(mu_ok, 1)
            with act.Fori(0, KC) as k:
                act.wait_ge(xc_ok, k + 1)
                squares(1, k, cv[:, k, :])
            root(1)
            with act.Fori(0, KC) as k:
                act.wait_ge(ln_t, k + 1)
                apart(act)
                act.activation(cv[:, k, :], cv[:, k, :], ACT.Silu, bias=col("conv_ln_b", k),
                               scale=col("conv_ln_g", k)).then_inc(ln_y, 1)
                act.wait_ge(ln_y, k + 1)
                apart(act)
                act.activation(Sh[:, k, :], cv[:, k, :], ACT.Copy).then_inc(s_hi, 1)

            with act.Fori(0, KC // RING) as i:
                for s in range(RING):
                    w_split(TURN_PW2 + i, s)
            act.wait_ge(mm, n_half(TURN_FFN0 - 1, RING - 1, 1))
            renorm(2, 0, 2 * KC, "ffn_norm_g", 0)

            def ffn(layer, turn0):
                off = HEADS * RING * layer

                def group(g, size, turn):
                    with act.Fori(0, size // 2) as i:
                        for cc in range(2):
                            for s in range(2):
                                w_split(turn + i, 2 * cc + s, off)
                            m = (g * GROUP + 2 * i + cc) * 2 + 2 * FC * layer
                            for hf in range(2):
                                act.wait_ge(t1_ok, m + (hf + 1))
                                act.activation(tmp[:, hf, 0, :], tmp[:, hf, 0, :], ACT.Silu).then_inc(silu_ok, 1)
                            for hf in range(2):
                                act.wait_ge(hid_t, m + (hf + 1))
                                apart(act)
                                act.activation(Gh[:, 2 * i + cc, hf * HT:(hf + 1) * HT], tmp[:, hf, 1, :],
                                               ACT.Copy).then_inc(hid_hi, 1)

                    def down(i, splits):
                        for s in range(splits):
                            w_split(turn + size // 2 + i, s, off)

                    if layer == 1 and size == REST:
                        for i in range(KC // RING):
                            down(i, RING if i + 1 < KC // RING else RING - 2)
                    else:
                        with act.Fori(0, KC // RING) as i:
                            down(i, RING)

                with act.Fori(0, GROUPS) as g:
                    group(g, GROUP, turn0 + g * GROUP_TURNS)
                group(GROUPS, REST, turn0 + GROUPS * GROUP_TURNS)

            ffn(0, TURN_FFN0)
            renorm(3, KC, 3 * KC, None)

            def att_split(h, r, used_sem, used, slot=None):
                act.wait_ge(raw_ok, att_block(h, r) + 1)
                act.wait_ge(used_sem, used)
                act.activation(flat(Wh[SLOT[r] if slot is None else slot]), flat(raw[att_stage(r)]),
                               ACT.Copy).then_inc(w_hi, 1)

            def split_qk(h):
                act.wait_ge(pj_ev, h * 6 + 5)
                if not isinstance(h, int) or h > 0:
                    act.wait_ge(s_mm, h * (2 * TB))
                act.activation(Qh[:, :], qS[:, :], ACT.Copy).then_inc(qk_hi, 1)
                act.activation(Kh[:, :], kS[:, :], ACT.Copy).then_inc(qk_hi, 1)

            def exps(h, i, c):
                w = (i + 1) * P
                act.wait_ge(s_ev, h * (2 * TB) + (2 * i + c + 3))
                v = (sc1[:, 0:w] if c else sc0[:, i % 2, 0:w])
                m = 2 * (i % 2) + c
                act.activation(v, v, ACT.Exp, bias=negmax[:, m:m + 1], scale=-1.0,
                               accum_out=rowsum[:, m:m + 1]).then_inc(e_ok, 1)

            def v_split(h, n):
                act.wait_ge(tr_mm, h * TR + (n + 1))
                act.activation(flat(Vh[:, 4 * n:4 * n + 4, :]), ps[:, 6, :], ACT.Copy).then_inc(tr_hi, 1)

            def weights_split(h, i, n):
                j0 = 4 * n
                nj = min(4, i + 1 - j0)
                act.wait_ge(tr_mm, h * TR + (TR_AT[i] + n + 1))
                act.activation(ATh[:, j0:j0 + nj, (i % 2) * P:(i % 2 + 1) * P],
                               ps[:, 6, 0:nj * P].rearrange("p (j q) -> p j q", q=P), ACT.Copy).then_inc(tr_hi, 1)

            def out_square(h, hf):
                act.wait_ge(pv_mm, h * 4 + (2 * hf + 2))
                act.activation(ob, ps[:, 7, :], ACT.Square).then_inc(osq_ok, 1)

            def out_root(h, hf):
                act.wait_ge(ov_mm, h * 2 + (hf + 1))
                act.activation(rb, ps[:, 1, :], ACT.Sqrt, bias=eps, scale=1.0 / P).then_inc(ostd_ok, 1)

            def out_hi(h, hf):
                act.wait_ge(o_ev, h * 2 + (hf + 2))
                act.activation(Oh[:, hf * HT:(hf + 1) * HT], ob, ACT.Copy, scale=sub_g).then_inc(o_hi, 1)

            def head(h, first=False, last=False):
                for i in range(TB):
                    more = i + 1 < TB
                    if i == 1 and not first:
                        out_root(h - 1, 1)
                    if i == 5:
                        out_root(h, 0)
                    if i == TB - 1 and not last:
                        split_qk(h + 1)
                    if more:
                        exps(h, i + 1, 0)
                    if i == 0:
                        v_split(h, 0)
                        if not first:
                            out_square(h - 1, 1)
                        if not last:
                            att_split(h, Q_R, pj_mm, h * 6 + 6)
                        exps(h, 1, 1)
                        v_split(h, 1)
                    weights_split(h, i, 0)
                    if more and i:
                        exps(h, i + 1, 1)
                    if i == 1 and not first:
                        out_hi(h - 1, 1)
                    if i == 2 and not last:
                        att_split(h, K_R, pj_mm, h * 6 + 4)
                    if i == 3 and not last:
                        att_split(h, V_R, pj_mm, h * 6 + 8)
                    if i >= 4:
                        weights_split(h, i, 1)
                    if i == 4:
                        out_square(h, 0)
                    if i == 5:
                        out_hi(h, 0)
                    if i == 6:
                        if first:
                            att_split(h, O_R, pj_mm, 1)
                        else:
                            att_split(h, 0 if last else O_R, wo_mm, h * 16, 3)
                if not last:
                    exps(h + 1, 0, 0)
                    exps(h + 1, 0, 1)

            act.wait_ge(raw_ok, ATT0 + 3)
            act.wait_ge(pj_mm, 2)
            act.activation(flat(Wh[0]), flat(raw[0]), ACT.Copy).then_inc(w_hi, 1)
            split_qk(0)
            exps(0, 0, 0)
            exps(0, 0, 1)
            head(0, first=True)
            with act.Fori(1, HEADS - 1) as h:
                head(h)
            head(HEADS - 1, last=True)
            out_square(HEADS - 1, 1)
            out_root(HEADS - 1, 1)
            out_hi(HEADS - 1, 1)
            for s in range(2):
                b = TURN_FFN1 * RING + s
                act.wait_ge(raw_ok, b + 1)
                act.activation(flat(Wh[s]), flat(raw[s]), ACT.Copy).then_inc(w_hi, 1)
            act.wait_ge(wo_ev, HEADS * 16 + 1)
            renorm(4, None, 4 * KC, "ffn_norm_g", KC)
            ffn(1, TURN_FFN1)

            with act.Fori(0, KC) as k:
                act.wait_ge(x_ok, k + (2 * KC + 1))
                squares(5, k, xT[:, k, :])
            root(5)
            for t in range(TB):
                act.wait_ge(yt_mm, t + 1)
                act.activation(yout[:, t, :], flat(ps[:, 2 * (t % 4):2 * (t % 4) + 2, :]),
                               ACT.Copy).then_inc(yt_ev, 1)

        @block.vector
        def _(dve):
            dve.sem_inc(rel, RING)
            dve.sem_inc(s_ev, 2)
            for ev in (pj_ev, tr_ev, o_ev, wo_ev):
                dve.sem_inc(ev, 1)

            def w_lo_of(turn, s):
                t2, s2 = turn + (s + 2) // RING, (s + 2) % RING
                dve.wait_ge(w_hi, n_block(t2, s2))
                dve.tensor_tensor(flat(Wl[s2]), flat(raw[s2 % 2]), flat(Wh[s2]).bitcast(F32),
                                  ALU.subtract).then_inc(w_lo, 1)

            def recip(n):
                for hf in range(2):
                    v = rstd[:, hf * HT:(hf + 1) * HT]
                    dve.wait_ge(std_ok, 2 * n + hf + 1)
                    dve.reciprocal(v, v).then_inc(rstd_ok, 1)
                dve.wait_ge(rstd_ok, 2 * n + 2)

            def renorm(n, base, gain, gain_at=0):
                with dve.Fori(0, KC) as k:
                    dve.wait_ge(s_hi, k + (base + 1))
                    g = 1.0 if gain is None else col(gain, gain_at + k)
                    dve.scalar_tensor_tensor(Sl[:, k, :], xT[:, k, :], g, Sh[:, k, :].bitcast(F32),
                                             ALU.mult, ALU.subtract).then_inc(s_lo, 1)
                recip(n)

            dve.wait_ge(vec_t, 3)
            dve.tensor_copy(vec[:, :], ps[:, 6, 0:NVEC]).then_inc(vec_ev, 1)
            dve.tensor_copy(dw[:, 0:DWR], ps[:, 7, 0:DWR]).then_inc(vec_ev, 1)
            dve.tensor_copy(dw[:, DWR:2 * DWR], ps[:, 7, P:P + DWR]).then_inc(vec_ev, 1)
            dve.wait_ge(vec_in, 16 * (len(VECS) + 5))
            dve.tensor_tensor(lpair[:, :, :], lamv[:, 0:4:2, :], lamv[:, 1:4:2, :], ALU.mult).then_inc(lam_s, 1)
            dve.wait_ge(lam_s, 1)
            dve.tensor_reduce(lsum, lpair[:, :, :], AX_X, ALU.add).then_inc(lam_s, 1)
            dve.wait_ge(lam_e, 1)
            dve.tensor_tensor(neg_lam, lexp[:, 1:2], lexp[:, 0:1], ALU.subtract).then_inc(lam_s, 1)
            dve.wait_ge(lam_s, 3)
            dve.tensor_scalar(neg_lam, neg_lam, -LAMBDA_INIT, None, ALU.add).then_inc(lam_s, 1)
            dve.wait_ge(vec_ev, 3)
            dve.tensor_scalar(sub_g, col("subln_g"), 1.0 - LAMBDA_INIT, None, ALU.mult).then_inc(lam_s, 1)
            for b in range(2):
                dve.wait_ge(w_hi, b + 1)
                dve.tensor_tensor(flat(Wl[b]), flat(raw[b]), flat(Wh[b]).bitcast(F32), ALU.subtract).then_inc(w_lo, 1)
            renorm(0, 0, "conv_norm_g")

            dve.memset(up[:, :, 0:PAD], 0.0).then_inc(glu_ok, 1)

            PER = DVE_TAPS + 1
            def pw1_pair(turn, n, cc):
                w_lo_of(turn, 2 * cc)
                w_lo_of(turn, 2 * cc + 1)
                val, gate = 4 * cc, 4 * cc + 2
                for hf in range(2):
                    dve.wait_ge(mm, n_half(turn, 2 * cc + 1, hf))
                    r = rstd[:, hf * HT:(hf + 1) * HT]
                    dve.tensor_tensor(tmp[:, hf, 0, :], ps[:, gate + hf, :], r, ALU.mult).then_inc(gate_t, 1)
                    dve.tensor_tensor(tmp[:, hf, 1, :], ps[:, val + hf, :], r, ALU.mult).then_inc(val_t, 1)
                for hf in range(2):
                    dve.wait_ge(val_t, n * 2 + (hf + 1))
                    dve.wait_ge(gate_s, n * 2 + (hf + 1))
                    dve.scalar_tensor_tensor(up[:, cc, PAD + hf * HT:PAD + (hf + 1) * HT], tmp[:, hf, 1, :],
                                             col("pw1_b", n), tmp[:, hf, 0, :], ALU.add, ALU.mult).then_inc(glu_ok, 1)
                dve.sem_inc(rel, 2)
                dve.wait_ge(glu_ok, n * 2 + 3)
                o = cv[:, n, :]
                for m in range(DVE_TAPS):
                    j = ACT_TAPS + m
                    wj = dw[:, bass.ds(j * KC + n, 1)]
                    src = up[:, cc, j:j + T]
                    if m == 0:
                        dve.tensor_scalar(o, src, wj, col("dw_b", n), ALU.mult, ALU.add).then_inc(conv_s, 1)
                    else:
                        dve.wait_ge(conv_s, n * DVE_TAPS + m)
                        dve.scalar_tensor_tensor(o, src, wj, o, ALU.mult, ALU.add).then_inc(conv_s, 1)
                dve.wait_ge(conv_s, n * DVE_TAPS + DVE_TAPS)
                dve.wait_ge(tap_ok, n * (ACT_TAPS - 1) + (ACT_TAPS - 1))
                dve.tensor_tensor(o, o, cacc[:, :], ALU.add).then_inc(cv_ok, 1)

            with dve.Fori(0, KC // 2) as i:
                for cc in range(2):
                    pw1_pair(i, 2 * i + cc, cc)

            dve.wait_ge(mu_ok, 2)
            dve.wait_ge(cv_ok, KC)
            with dve.Fori(0, KC) as k:
                dve.tensor_tensor(cv[:, k, :], cv[:, k, :], mu[:, :], ALU.subtract).then_inc(xc_ok, 1)
            recip(1)
            with dve.Fori(0, KC) as k:
                dve.wait_ge(xc_ok, k + 1)
                dve.tensor_tensor(cv[:, k, :], cv[:, k, :], rstd[:, :], ALU.mult).then_inc(ln_t, 1)
            with dve.Fori(0, KC) as k:
                dve.wait_ge(s_hi, k + (KC + 1))
                dve.tensor_tensor(Sl[:, k, :], cv[:, k, :], Sh[:, k, :].bitcast(F32), ALU.subtract).then_inc(s_lo, 1)

            with dve.Fori(0, KC // RING) as i:
                for s in range(RING):
                    w_lo_of(TURN_PW2 + i, s)
                    n = RING * i + s
                    for hf in range(2):
                        xs = xT[:, n, hf * HT:(hf + 1) * HT]
                        dve.wait_ge(mm, n_half(TURN_PW2 + i, s, hf))
                        ins = dve.scalar_tensor_tensor(xs, ps[:, 2 * s + hf, :], col("pw2_b", n), xs, ALU.add, ALU.add)
                    ins.then_inc(x_ok, 1)
                    dve.wait_ge(x_ok, n + 1)
                    dve.sem_inc(rel, 1)
            renorm(2, 2 * KC, "ffn_norm_g", 0)

            def ffn(layer, turn0, x_base):
                off = HEADS * RING * layer

                def group(g, size, turn, last):
                    with dve.Fori(0, size // 2) as i:
                        for cc in range(2):
                            b1, b3 = 4 * cc, 4 * cc + 2
                            m = (g * GROUP + 2 * i + cc) * 2 + 2 * FC * layer
                            w_lo_of(turn + i, 2 * cc)
                            for hf in range(2):
                                dve.wait_ge(mm, n_half(turn + i, 2 * cc, hf, off))
                                dve.tensor_tensor(tmp[:, hf, 0, :], ps[:, b1 + hf, :], rstd[:, hf * HT:(hf + 1) * HT],
                                                  ALU.mult).then_inc(t1_ok, 1)
                            w_lo_of(turn + i, 2 * cc + 1)

                            def lo(hf):
                                cs = slice(hf * HT, (hf + 1) * HT)
                                dve.wait_ge(hid_hi, m + (hf + 1))
                                dve.tensor_tensor(Gl[:, 2 * i + cc, cs], tmp[:, hf, 1, :],
                                                  Gh[:, 2 * i + cc, cs].bitcast(F32), ALU.subtract).then_inc(hid_lo, 1)

                            for hf in range(2):
                                dve.wait_ge(mm, n_half(turn + i, 2 * cc + 1, hf, off))
                                dve.tensor_tensor(tmp[:, hf, 1, :], ps[:, b3 + hf, :], rstd[:, hf * HT:(hf + 1) * HT],
                                                  ALU.mult).then_inc(t3_ok, 1)
                                dve.wait_ge(t3_ok, m + (hf + 1))
                                dve.wait_ge(silu_ok, m + (hf + 1))
                                dve.tensor_tensor(tmp[:, hf, 1, :], tmp[:, hf, 1, :], tmp[:, hf, 0, :],
                                                  ALU.mult).then_inc(hid_t, 1)
                                if hf:
                                    dve.sem_inc(rel, 2)
                                    lo(0)
                            lo(1)
                            dve.wait_ge(hid_lo, m + 2)

                    def down(i, splits):
                        for s in range(RING):
                            if s < splits:
                                w_lo_of(turn + size // 2 + i, s)
                            n = RING * i + s
                            for hf in range(2):
                                xs = xT[:, n, hf * HT:(hf + 1) * HT]
                                dve.wait_ge(mm, n_half(turn + size // 2 + i, s, hf, off))
                                ins = dve.tensor_tensor(xs, ps[:, 2 * s + hf, :], xs, ALU.add)
                                if hf:
                                    ins.then_inc(x_ok if last else rel, 1)
                            if last:
                                dve.wait_ge(x_ok, n + (x_base + 1))
                                dve.sem_inc(rel, 1)

                    if layer == 1 and last:
                        for i in range(KC // RING):
                            down(i, RING if i + 1 < KC // RING else RING - 2)
                    else:
                        with dve.Fori(0, KC // RING) as i:
                            down(i, RING)

                with dve.Fori(0, GROUPS) as g:
                    group(g, GROUP, turn0 + g * GROUP_TURNS, False)
                group(GROUPS, REST, turn0 + GROUPS * GROUP_TURNS, True)

            ffn(0, TURN_FFN0, KC)
            renorm(3, 3 * KC, None)

            ATT_STEPS = 3 * TB

            def att_lo(h, r, slot=None):
                sl = SLOT[r] if slot is None else slot
                dve.wait_ge(w_hi, att_block(h, r) + 1)
                dve.tensor_tensor(flat(Wl[sl]), flat(raw[att_stage(r)]), flat(Wh[sl]).bitcast(F32),
                                  ALU.subtract).then_inc(w_lo, 1)

            def projected(h, m):
                cs = slice(m % 2 * HT, (m % 2 + 1) * HT)
                dve.wait_ge(pj_mm, h * 6 + (m + 1))
                if m == 4 and not (isinstance(h, int) and h == 0):
                    dve.wait_ge(o_lo, h * 2 - 1)
                if m < 2:
                    dve.scalar_tensor_tensor(qS[:, cs], ps[:, 0, :], Q_SHIFT, rstd[:, cs],
                                             ALU.mult, ALU.mult).then_inc(pj_ev, 1)
                else:
                    dve.tensor_tensor((kS, vS)[m // 2 - 1][:, cs], ps[:, 0, :], rstd[:, cs],
                                      ALU.mult).then_inc(pj_ev, 1)

            def qk_low(h):
                for n, (lo, hi, st) in enumerate(((Ql, Qh, qS), (Kl, Kh, kS))):
                    dve.wait_ge(qk_hi, h * 2 + (n + 1))
                    dve.tensor_tensor(lo[:, :], st[:, :], hi[:, :].bitcast(F32), ALU.subtract).then_inc(qk_lo, 1)

            def score_rows(h, i, c):
                w = (i + 1) * P
                b0 = (TB - 1 - i) * P
                dve.wait_ge(s_mm, h * (2 * TB) + (2 * i + c + 1))
                if c and i:
                    dve.wait_ge(a_ok, h * TB + i)
                apart(dve)
                m = 2 * (i % 2) + c
                dve.tensor_tensor_reduce(sc1[:, 0:w] if c else sc0[:, i % 2, 0:w],
                                         flat(ps[:, 2 + 2 * c:4 + 2 * c, :])[:, 0:w], bias[:, b0:b0 + w],
                                         -QK_SCALE / Q_SHIFT, 3e38, ALU.add, ALU.min, negmax[:, m:m + 1]).then_inc(s_ev, 1)

            def att_weights(h, i):
                w = (i + 1) * P
                p0 = sc0[:, i % 2, 0:w]
                m = 2 * (i % 2)
                dve.wait_ge(e_ok, h * (2 * TB) + (2 * i + 2))
                dve.reciprocal(rrow, rowsum[:, m:m + 2]).then_inc(att_s, 1)
                dve.wait_ge(att_s, h * ATT_STEPS + (3 * i + 1))
                dve.tensor_tensor(rlam, rrow[:, 1:2], neg_lam, ALU.mult).then_inc(att_s, 1)
                dve.wait_ge(att_s, h * ATT_STEPS + (3 * i + 2))
                dve.tensor_scalar(sc1[:, 0:w], sc1[:, 0:w], rlam, None, ALU.mult).then_inc(att_s, 1)
                dve.wait_ge(att_s, h * ATT_STEPS + (3 * i + 3))
                dve.scalar_tensor_tensor(p0, p0, rrow[:, 0:1], sc1[:, 0:w], ALU.mult, ALU.add).then_inc(a_ok, 1)

            def v_low(h, n):
                dve.wait_ge(tr_hi, h * TR + (n + 1))
                dve.tensor_tensor(flat(Vl[:, 4 * n:4 * n + 4, :]), ps[:, 6, :],
                                  flat(Vh[:, 4 * n:4 * n + 4, :]).bitcast(F32), ALU.subtract).then_inc(tr_ev, 1)

            def weights_low(h, i, n):
                j0 = 4 * n
                nj = min(4, i + 1 - j0)
                qs = slice((i % 2) * P, (i % 2 + 1) * P)
                dve.wait_ge(tr_hi, h * TR + (TR_AT[i] + n + 1))
                dve.tensor_tensor(ATl[:, j0:j0 + nj, qs], ps[:, 6, 0:nj * P].rearrange("p (j q) -> p j q", q=P),
                                  ATh[:, j0:j0 + nj, qs].bitcast(F32), ALU.subtract).then_inc(tr_ev, 1)

            def out_recip(h, hf, part):
                v = rb[:, part * (HT // 2):(part + 1) * (HT // 2)]
                dve.wait_ge(ostd_ok, h * 2 + (hf + 1))
                dve.reciprocal(v, v).then_inc(orec_ok, 1)

            def out_norm(h, hf):
                dve.wait_ge(orec_ok, h * 4 + (2 * hf + 2))
                dve.tensor_tensor(ob, ps[:, 7, :], rb, ALU.mult).then_inc(o_ev, 1)

            def out_low(h, hf):
                cs = slice(hf * HT, (hf + 1) * HT)
                dve.wait_ge(o_hi, h * 2 + (hf + 1))
                dve.scalar_tensor_tensor(Ol[:, cs], ob, sub_g, Oh[:, cs].bitcast(F32),
                                         ALU.mult, ALU.subtract).then_inc(o_lo, 1)

            def add_out(h, m, bank):
                hf, n = m // KC, m % KC
                xs = xT[:, n, hf * HT:(hf + 1) * HT]
                dve.wait_ge(wo_mm, h * 16 + (m + 1))
                dve.tensor_tensor(xs, ps[:, bank, :], xs, ALU.add).then_inc(wo_ev, 1)

            def head(h, first=False, last=False):
                def on_p(m, k):
                    if k == KC - 1 and not last:
                        projected(h + 1, m)

                def on_w(dh, m):
                    if dh == 0:
                        add_out(h, m, 1)
                    elif not first:
                        add_out(h - 1, m, 1)

                for i in range(TB):
                    more = i + 1 < TB
                    if more:
                        score_rows(h, i + 1, 0)
                    att_weights(h, i)
                    if i == TB - 1 and not last:
                        qk_low(h + 1)
                    if i == 2 and not first:
                        out_low(h - 1, 1)
                    if i == 6:
                        out_low(h, 0)
                    beside(i, 0, on_p, on_w)
                    if i == 0:
                        v_low(h, 0)
                    if more:
                        score_rows(h, i + 1, 1)
                    if i == 0:
                        v_low(h, 1)
                    beside(i, 1, on_p, on_w)
                    if i == 1 and not first:
                        out_recip(h - 1, 1, 0)
                    if i == 5:
                        out_recip(h, 0, 0)
                    weights_low(h, i, 0)
                    if i == 1 and not first:
                        out_recip(h - 1, 1, 1)
                        out_norm(h - 1, 1)
                    if i == 5:
                        out_recip(h, 0, 1)
                        out_norm(h, 0)
                    if i == 0 and not last:
                        att_lo(h, Q_R)
                    beside(i, 2, on_p, on_w)
                    if i == 2 and not last:
                        att_lo(h, K_R)
                    if i == 3 and not last:
                        att_lo(h, V_R)
                    if i >= 4:
                        weights_low(h, i, 1)
                    if i == 6:
                        att_lo(h, 0 if last else O_R, 3)
                    beside(i, 3, on_p, on_w)
                if not last:
                    dve.wait_ge(bias_ok, 2 * h + 6)
                    score_rows(h + 1, 0, 0)
                    score_rows(h + 1, 0, 1)

            for m in range(6):
                projected(0, m)
                if m == 1:
                    att_lo(0, -1, 0)
            qk_low(0)
            dve.wait_ge(bias_ok, 4)
            score_rows(0, 0, 0)
            score_rows(0, 0, 1)
            head(0, first=True)
            with dve.Fori(1, HEADS - 1) as h:
                head(h)
            head(HEADS - 1, last=True)
            for m in range(EARLY, KC):
                add_out(HEADS - 1, m, 2 + m % 4)
            out_recip(HEADS - 1, 1, 0)
            out_recip(HEADS - 1, 1, 1)
            out_norm(HEADS - 1, 1)
            out_low(HEADS - 1, 1)
            for s in range(2):
                b = TURN_FFN1 * RING + s
                dve.wait_ge(w_hi, b + 1)
                dve.tensor_tensor(flat(Wl[s]), flat(raw[s]), flat(Wh[s]).bitcast(F32), ALU.subtract).then_inc(w_lo, 1)
            for m in range(KC, 2 * KC):
                add_out(HEADS - 1, m, 2 + m % 4)
            renorm(4, 4 * KC, "ffn_norm_g", KC)
            ffn(1, TURN_FFN1, 2 * KC)

            recip(5)
            for hf in range(2):
                cs = slice(hf * HT, (hf + 1) * HT)
                for k in range(KC):
                    dve.scalar_tensor_tensor(xT[:, k, cs], xT[:, k, cs], col("final_norm_g", k), rstd[:, cs],
                                             ALU.mult, ALU.mult).then_inc(y_ok, 1)

        @block.tensor
        def _(pe):
            def transpose(dst, src, m=P):
                return pe.transpose(dst, src, ident[0:m, 0:m])

            pe.wait_ge(consts, 4)
            pe.wait_ge(vec_in, 16 * (len(VECS) + 5))
            transpose(ps[:, 6, 0:NVEC], vrow[0:NVEC, :], NVEC).then_inc(vec_t, 1)
            for s in range(2):
                transpose(ps[:, 7, s * P:s * P + DWR], dwrow[:, s, :], DWR).then_inc(vec_t, 1)
            for t in range(TB):
                pe.wait_ge(x_in[t], 16)
                if t == 3:
                    pe.wait_ge(vec_ev, 3)
                if t >= 4:
                    pe.wait_ge(xt_ev, t - 3)
                for k in range(KC):
                    ins = transpose(ps[:, 2 * (t % 4) + k // 4, (k % 4) * P:(k % 4 + 1) * P],
                                    xrow[:, t, k * P:(k + 1) * P])
                ins.then_inc(xt_mm, 1)

            def product(dst, lh, ll, rh, rl, start, stop):
                pe.matmul(dst, ll, rh, start=start, stop=False)
                pe.matmul(dst, lh, rl, start=False, stop=False)
                return pe.matmul(dst, lh, rh, start=False, stop=stop)

            def dense(turn, s, src_h, src_l, chunks, rel_off=0, ready=None, bank=None):
                pe.wait_ge(w_lo, n_block(turn, s))
                if bank is None:
                    pe.wait_ge(rel, n_rel(turn, s) - rel_off)
                for hf in range(2):
                    cs = slice(hf * HT, (hf + 1) * HT)
                    dst = ps[:, (2 * s if bank is None else bank) + hf, :]
                    for k in range(chunks):
                        if ready is not None:
                            ready(hf, k)
                        ins = product(dst, Wh[s][:, k, :], Wl[s][:, k, :], src_h[:, k, cs], src_l[:, k, cs],
                                      k == 0, k == chunks - 1)
                    ins.then_inc(mm, 1)

            def variance(n):
                pe.wait_ge(acc_ok, (KC + 1) * (n + 1))
                for hf in range(2):
                    pe.matmul(ps[:, var_bank[n] + hf, :], ones[:, :], acc[:, hf * HT:(hf + 1) * HT],
                              start=True, stop=True).then_inc(var_mm, 1)

            def s_ready(base):
                def ready(hf, k):
                    if hf == 0:
                        pe.wait_ge(s_lo, base + k + 1)
                return ready

            pe.wait_ge(xt_ev, TB)
            dense(0, 0, Sh, Sl, KC, ready=s_ready(0))
            dense(0, 1, Sh, Sl, KC)
            variance(0)
            dense(0, 2, Sh, Sl, KC)
            pe.wait_ge(std_ok, 2)
            dense(0, 3, Sh, Sl, KC)
            with pe.Fori(1, 2 * KC // RING) as i:
                for s in range(RING):
                    dense(i, s, Sh, Sl, KC)

            pe.wait_ge(rel, TURN_PW2 * RING + RING)
            for k in range(KC):
                pe.wait_ge(cv_ok, k + 1)
                for hf in range(2):
                    ins = pe.matmul(ps[:, hf, :], ones[:, :], cv[:, k, hf * HT:(hf + 1) * HT],
                                    start=k == 0, stop=k == KC - 1)
                    if k == KC - 1:
                        ins.then_inc(mean_mm, 1)
            variance(1)

            dense(TURN_PW2, 0, Sh, Sl, KC, ready=s_ready(KC))
            for s in range(1, RING):
                dense(TURN_PW2, s, Sh, Sl, KC)
            with pe.Fori(1, KC // RING) as i:
                for s in range(RING):
                    dense(TURN_PW2 + i, s, Sh, Sl, KC)

            def ffn(layer, turn0, n, s_base, off):
                def up_turn(turn, first=False):
                    for s in range(RING):
                        if first and s == 2:
                            variance(n)
                        if first and s == 3:
                            pe.wait_ge(std_ok, 2 * n + 2)
                        dense(turn, s, Sh, Sl, KC, off, s_ready(s_base) if first and s == 0 else None)

                def down(g, size, turn):
                    base = 2 * FC * layer + 1

                    def ready(hf, k):
                        pe.wait_ge(hid_lo, g * (2 * GROUP) + (base + 2 * k + hf))
                    with pe.Fori(0, KC // RING) as i:
                        for s in range(RING):
                            dense(turn + i, s, Gh, Gl, size, off, ready if s == 0 else None)

                up_turn(turn0, True)
                with pe.Fori(1, GROUP // 2) as i:
                    up_turn(turn0 + i)
                down(0, GROUP, turn0 + GROUP // 2)
                with pe.Fori(1, GROUPS) as g:
                    with pe.Fori(0, GROUP // 2) as i:
                        up_turn(turn0 + g * GROUP_TURNS + i)
                    down(g, GROUP, turn0 + g * GROUP_TURNS + GROUP // 2)
                turn = turn0 + GROUPS * GROUP_TURNS
                with pe.Fori(0, REST // 2) as i:
                    up_turn(turn + i)
                down(GROUPS, REST, turn + REST // 2)

            ffn(0, TURN_FFN0, 2, 2 * KC, 0)

            pe.wait_ge(rel, TURN_ATT * RING + RING)
            variance(3)

            def project(h, m, k0, k1, ready=None):
                slot = (0, 1, 0)[m // 2]
                cs = slice(m % 2 * HT, (m % 2 + 1) * HT)
                for k in range(k0, k1):
                    if ready is not None:
                        pe.wait_ge(s_lo, ready + k + 1)
                    ins = product(ps[:, 0, :], Wh[slot][:, k, :], Wl[slot][:, k, :], Sh[:, k, cs], Sl[:, k, cs],
                                  k == 0, k == KC - 1)
                if k1 == KC:
                    ins.then_inc(pj_mm, 1)

            def scores(h, i, c):
                qs = slice(i * P, (i + 1) * P)
                cp = slice(c * HD, (c + 1) * HD)
                pe.wait_ge(s_ev, h * (2 * TB) + (2 * i + c + 1))
                for n0 in range(0, (i + 1) * P, HT):
                    n1 = min((i + 1) * P, n0 + HT)
                    ins = product(ps[:, 2 + 2 * c + n0 // HT, 0:n1 - n0], Qh[cp, qs], Ql[cp, qs],
                                  Kh[cp, n0:n1], Kl[cp, n0:n1], True, True)
                ins.then_inc(s_mm, 1)

            def v_turn(h, n):
                pe.wait_ge(pj_ev, h * 6 + (5 + n + 1))
                pe.wait_ge(tr_ev, h * TR + (n + 1))
                for j in range(4):
                    ins = transpose(ps[:, 6, j * P:(j + 1) * P], vS[:, (4 * n + j) * P:(4 * n + j + 1) * P])
                ins.then_inc(tr_mm, 1)

            def weights_turn(h, i, n):
                pe.wait_ge(a_ok, h * TB + (i + 1))
                pe.wait_ge(tr_ev, h * TR + (TR_AT[i] + n + 1))
                for j in range(4 * n, min(4 * n + 4, i + 1)):
                    ins = transpose(ps[:, 6, (j - 4 * n) * P:(j - 4 * n + 1) * P], sc0[:, i % 2, j * P:(j + 1) * P])
                ins.then_inc(tr_mm, 1)

            def values(h, pair):
                i = 2 * pair + 1
                q0 = pair % 2 * 2 * P
                pe.wait_ge(tr_ev, h * TR + (TR_AT[i] + i // 4 + 2))
                if pair % 2 == 0:
                    pe.wait_ge(o_ev, h * 2 + (pair // 2 + 1))
                for j in range(i + 1):
                    c0 = P if j == i else 0
                    ins = product(ps[:, 7, q0 + c0:q0 + 2 * P], Vh[:, j, :], Vl[:, j, :],
                                  ATh[:, j, c0:2 * P], ATl[:, j, c0:2 * P], j == 0, j == i)
                ins.then_inc(pv_mm, 1)

            def out_sum(h, hf, before):
                pe.wait_ge(osq_ok, h * 2 + (hf + 1))
                pe.wait_ge(wo_ev, before)
                pe.matmul(ps[:, 1, :], ones[:, :], ob, start=True, stop=True).then_inc(ov_mm, 1)

            def unit(h, m, bank=1):
                hf, n = m // KC, m % KC
                cs = slice(hf * HT, (hf + 1) * HT)
                if m % KC == 0:
                    pe.wait_ge(o_lo, h * 2 + (hf + 1))
                pe.wait_ge(wo_ev, h * 16 + (m + 1 if bank == 1 else m - 2))
                product(ps[:, bank, :], Wh[3][:, n, :], Wl[3][:, n, :], Oh[:, cs], Ol[:, cs], True, True) \
                    .then_inc(wo_mm, 1)

            def head(h, first=False, last=False):
                def on_p(m, k):
                    if last:
                        return
                    if k == 0:
                        if m % 2 == 0:
                            pe.wait_ge(w_lo, att_block(h, Q_R + m // 2) + 1)
                        pe.wait_ge(pj_ev, h * 6 + (6 + m + 1))
                    project(h + 1, m, k, k + 1)

                def on_w(dh, m):
                    if dh == 0:
                        if m == 0:
                            pe.wait_ge(w_lo, att_block(h, 0 if last else O_R) + 1)
                        unit(h, m)
                    elif not first:
                        unit(h - 1, m)

                for i in range(TB):
                    if i == 1 and not first:
                        out_sum(h - 1, 1, h * 16 - 15 + units_before(1))
                        pe.wait_ge(ostd_ok, h * 2)
                    if i == 5:
                        out_sum(h, 0, 1 if first else h * 16 - 15 + units_before(5))
                    if i + 1 < TB:
                        scores(h, i + 1, 0)
                    beside(i, 0, on_p, on_w)
                    if i == 5:
                        pe.wait_ge(ostd_ok, h * 2 + 1)
                    if i == 0:
                        if not first:
                            values(h - 1, 3)
                        v_turn(h, 0)
                    if i + 1 < TB:
                        scores(h, i + 1, 1)
                    if i == 0:
                        v_turn(h, 1)
                    if i % 2 == 0 and i:
                        values(h, i // 2 - 1)
                    beside(i, 1, on_p, on_w)
                    weights_turn(h, i, 0)
                    beside(i, 2, on_p, on_w)
                    if i >= 4:
                        weights_turn(h, i, 1)
                    beside(i, 3, on_p, on_w)
                if not last:
                    first_scores(h + 1)

            def first_scores(h):
                pe.wait_ge(qk_lo, h * 2 + 2)
                scores(h, 0, 0)
                scores(h, 0, 1)

            for m in range(6):
                if m % 2 == 0:
                    pe.wait_ge(w_lo, ATT0 + m // 2 + 1)
                pe.wait_ge(pj_ev, m + 1)
                project(0, m, 0, KC, 3 * KC if m == 0 else None)
            first_scores(0)
            head(0, first=True)
            with pe.Fori(1, HEADS - 1) as h:
                head(h)
            head(HEADS - 1, last=True)
            values(HEADS - 1, 3)
            pe.wait_ge(s_ev, HEADS * 2 * TB + 2)
            for m in range(EARLY, KC):
                unit(HEADS - 1, m, 2 + m % 4)
            out_sum(HEADS - 1, 1, HEADS * 16 - 15 + EARLY)
            for m in range(KC, 2 * KC):
                unit(HEADS - 1, m, 2 + m % 4)
            pe.wait_ge(wo_ev, HEADS * 16 + 1)
            ffn(1, TURN_FFN1, 4, 4 * KC, HEADS * RING)

            pe.wait_ge(rel, (TURNS - HEADS) * RING + RING)
            variance(5)
            for t in range(TB):
                pe.wait_ge(y_ok, KC * (t // 4 + 1))
                if t == 3:
                    pe.wait_ge(std_ok, 12)
                if t >= 4:
                    pe.wait_ge(yt_ev, t - 3)
                for k in range(KC):
                    ins = transpose(ps[:, 2 * (t % 4) + k // 4, (k % 4) * P:(k % 4 + 1) * P],
                                    xT[:, k, t * P:(t + 1) * P])
                ins.then_inc(yt_mm, 1)


var_bank = {0: 6, 1: 2, 2: 6, 3: 6, 4: 6, 5: 6}

_INS = ["x", "conv_norm_g", "pw1_w", "pw1_b", "dw_w", "dw_b", "conv_ln_g", "conv_ln_b", "pw2_w", "pw2_b", "kv_norm_g",
        "w_k", "w_v", "attn_norm_g", "w_q", "lambda_q1", "lambda_k1", "lambda_q2", "lambda_k2", "subln_g", "w_o",
        "ffn_norm_g", "ffn_w1", "ffn_w3", "ffn_w2", "final_norm_g"]


def kernel(**inputs):
    import numpy as _np
    import concourse.bacc as _bacc
    from concourse import mybir as _mybir
    from concourse.bass_utils import run_bass_kernel_spmd as _run

    nc = _bacc.Bacc("TRN2", target_bir_lowering=False, num_devices=1)
    arrays, args = {}, {}
    for name in _INS:
        v = _np.ascontiguousarray(inputs[name])
        arrays[f"in_{name}_dram"] = v
        args[name] = nc.dram_tensor(f"in_{name}_dram", v.shape, _mybir.dt.from_np(v.dtype), kind="ExternalInput").ap()
    out = nc.dram_tensor("out_0_dram", (1, T, D), F32, kind="ExternalOutput").ap()
    trunk(nc, args, out)
    r = _run(nc, [arrays], core_ids=[0])
    return r.results[0]["out_0_dram"]
```
